# Optimizing a Trainium2 kernel written in Bass

```python
import jax, jax.numpy as jnp
from jax import lax
import numpy as np

D_MODEL = 2048
BATCH = 1
SEQ = 256
DEPTH = 2

EPS = 1e-5
ROPE_THETA = 500000.0
BLOCK = 128
NEG_INF = -1e30

SWA_WINDOW = 128
A_Q_HEADS = 16
A_KV_HEADS = 4
A_HEAD_DIM = 64
A_Q_COLS = A_Q_HEADS * A_HEAD_DIM
A_KV_COLS = A_KV_HEADS * A_HEAD_DIM
B_WIDTH = 1024
CONV_WIDTH = 3
IN0_SPLITS = [A_Q_COLS, A_Q_COLS + A_KV_COLS, A_Q_COLS + 2 * A_KV_COLS,
              A_Q_COLS + 2 * A_KV_COLS + B_WIDTH, A_Q_COLS + 2 * A_KV_COLS + 2 * B_WIDTH]
IN0_COLS = A_Q_COLS + 2 * A_KV_COLS + 3 * B_WIDTH
MIX0_WIDTH = A_Q_COLS + B_WIDTH

C_Q_RANK = 512
C_HEADS = 16
C_HEAD_DIM = 128
IDX_HEADS = 16
IDX_HEAD_DIM = 64
INDEX_TOPK = 256
IN1_SPLITS = [C_Q_RANK, C_Q_RANK + C_HEAD_DIM, C_Q_RANK + 2 * C_HEAD_DIM,
              C_Q_RANK + 2 * C_HEAD_DIM + IDX_HEAD_DIM]
IN1_COLS = C_Q_RANK + 2 * C_HEAD_DIM + IDX_HEAD_DIM + IDX_HEADS
UQ_COLS = C_HEADS * C_HEAD_DIM + IDX_HEADS * IDX_HEAD_DIM
MIX1_WIDTH = C_HEADS * C_HEAD_DIM

PEER_HEADS = 8
PEER_N_KEYS = 128
PEER_EXPERTS = PEER_N_KEYS * PEER_N_KEYS
PEER_TOPK = 16
PEER_QDIM = 256
PEER_HALF = PEER_QDIM // 2

kernel_name = 'hybrid_swa_conv_dsa_peer'

def rms_norm(x, g):
    xf = x.astype(jnp.float32)
    y = xf * lax.rsqrt(jnp.mean(xf * xf, axis=-1, keepdims=True) + EPS)
    return (y * g.astype(jnp.float32)).astype(x.dtype)

def partial_rope(x, positions):
    dh = x.shape[-1]
    rot = dh // 4
    half = rot // 2
    inv = ROPE_THETA ** (-jnp.arange(half, dtype=jnp.float32) * 2.0 / rot)
    ang = positions.astype(jnp.float32)[:, :, None, None] * inv
    cos, sin = jnp.cos(ang), jnp.sin(ang)
    xf = x.astype(jnp.float32)
    x1, x2, rest = xf[..., :half], xf[..., half:rot], xf[..., rot:]
    out = jnp.concatenate([x1 * cos - x2 * sin, x2 * cos + x1 * sin, rest], axis=-1)
    return out.astype(x.dtype)

def sliding_window_gqa(q, k, v, sinks):
    Bn, S, Hq, dh = q.shape
    Hkv = k.shape[2]
    G = Hq // Hkv
    nb = S // BLOCK
    qb = q.reshape(Bn, nb, BLOCK, Hkv, G, dh)

    def band(t):
        tb = jnp.pad(t, ((0, 0), (BLOCK, 0), (0, 0), (0, 0))).reshape(Bn, nb + 1, BLOCK, Hkv, dh)
        return jnp.concatenate([tb[:, :-1], tb[:, 1:]], axis=2)

    kb, vb = band(k), band(v)
    s = jnp.einsum('bnqhgd,bnkhd->bnhgqk', qb, kb).astype(jnp.float32) * (dh ** -0.5)
    qi = jnp.arange(BLOCK)[:, None]
    kj = jnp.arange(2 * BLOCK)[None, :]
    diff = qi + BLOCK - kj
    in_win = (diff >= 0) & (diff < SWA_WINDOW)
    kpos = jnp.arange(nb)[:, None, None] * BLOCK - BLOCK + kj[None]
    valid = in_win[None] & (kpos >= 0)
    s = jnp.where(valid[None, :, None, None], s, NEG_INF)
    sink = jnp.broadcast_to(
        sinks.astype(jnp.float32).reshape(Hkv, G)[None, None, :, :, None, None],
        s.shape[:-1] + (1,))
    p = jax.nn.softmax(jnp.concatenate([s, sink], axis=-1), axis=-1)[..., :-1]
    o = jnp.einsum('bnhgqk,bnkhd->bnqhgd', p.astype(v.dtype), vb)
    return o.reshape(Bn, S, Hq * dh)

def short_gated_conv(b_gate, c_gate, h, conv_w):
    z = c_gate * h
    W = z.shape[-1]
    y = lax.conv_general_dilated(
        z, conv_w[:, None, :].astype(z.dtype), window_strides=(1,),
        padding=((CONV_WIDTH - 1, 0),), dimension_numbers=('NWC', 'WIO', 'NWC'),
        feature_group_count=W)
    return b_gate * y

def even_mixer(x, positions, norm_g, w_in, sinks, conv_w, w_out):
    Bn, S, _ = x.shape
    h = rms_norm(x, norm_g)
    q, k, v, bg, cg, hx = jnp.split(h @ w_in, IN0_SPLITS, axis=-1)
    q = partial_rope(q.reshape(Bn, S, A_Q_HEADS, A_HEAD_DIM), positions)
    k = partial_rope(k.reshape(Bn, S, A_KV_HEADS, A_HEAD_DIM), positions)
    v = v.reshape(Bn, S, A_KV_HEADS, A_HEAD_DIM)
    a_out = sliding_window_gqa(q, k, v, sinks)
    b_out = short_gated_conv(bg, cg, hx, conv_w)
    return x + jnp.concatenate([a_out, b_out], axis=-1) @ w_out

def indexed_sparse_attention(q, k, v, iq, ik, iw):
    Bn, S, H, dh = q.shape
    nb = S // BLOCK
    k_sel = min(INDEX_TOPK, S // 4)
    key_pos = jnp.arange(S)

    def blockify(t):
        return jnp.moveaxis(t.reshape((Bn, nb, BLOCK) + t.shape[2:]), 1, 0)

    def one_block(args):
        qb, iqb, iwb, qpos = args
        logits = jnp.einsum('bqhd,bsd->bqhs', iqb, ik).astype(jnp.float32)
        score = jnp.einsum('bqh,bqhs->bqs', iwb.astype(jnp.float32), jax.nn.relu(logits))
        causal = key_pos[None, :] <= qpos[:, None]
        score = jnp.where(causal[None], score, NEG_INF)
        _, idx = lax.top_k(score, k_sel)
        kg = jax.vmap(lambda kk, ii: kk[ii])(k, idx)
        vg = jax.vmap(lambda vv, ii: vv[ii])(v, idx)
        sel_valid = idx <= qpos[None, :, None]
        s = jnp.einsum('bqhd,bqkd->bqhk', qb, kg).astype(jnp.float32) * (dh ** -0.5)
        s = jnp.where(sel_valid[:, :, None, :], s, NEG_INF)
        p = jax.nn.softmax(s, axis=-1)
        return jnp.einsum('bqhk,bqkd->bqhd', p.astype(vg.dtype), vg)

    qpos_all = jnp.arange(S).reshape(nb, BLOCK)
    out = lax.map(one_block, (blockify(q), blockify(iq), blockify(iw), qpos_all))
    return jnp.moveaxis(out, 0, 1).reshape(Bn, S, H * dh)

def odd_mixer(x, positions, norm_g, w_in, g_qa, w_uq, w_out):
    Bn, S, _ = x.shape
    h = rms_norm(x, norm_g)
    cq, k, v, ik, iw = jnp.split(h @ w_in, IN1_SPLITS, axis=-1)
    uq = rms_norm(cq, g_qa) @ w_uq
    q, iq = jnp.split(uq, [C_HEADS * C_HEAD_DIM], axis=-1)
    q = partial_rope(q.reshape(Bn, S, C_HEADS, C_HEAD_DIM), positions)
    k = partial_rope(k.reshape(Bn, S, 1, C_HEAD_DIM), positions)[:, :, 0]
    iq = partial_rope(iq.reshape(Bn, S, IDX_HEADS, IDX_HEAD_DIM), positions)
    ik = partial_rope(ik.reshape(Bn, S, 1, IDX_HEAD_DIM), positions)[:, :, 0]
    iw = iw * ((IDX_HEADS ** -0.5) * (IDX_HEAD_DIM ** -0.5))
    o = indexed_sparse_attention(q, k, v, iq, ik, iw)
    return x + o @ w_out

def peer_ffn(h, w_q, sub_keys, u, v):
    Bn, S, D = h.shape
    nb = (Bn * S) // BLOCK
    hb = h.reshape(nb, BLOCK, D)

    def one_block(xb):
        q = (xb @ w_q).reshape(BLOCK, PEER_HEADS, 2, PEER_HALF)
        s = jnp.einsum('thcd,hcnd->thcn', q, sub_keys).astype(jnp.float32)
        top_s, top_i = lax.top_k(s, PEER_TOPK)
        cand_s = top_s[:, :, 0, :, None] + top_s[:, :, 1, None, :]
        cand_i = top_i[:, :, 0, :, None] * PEER_N_KEYS + top_i[:, :, 1, None, :]
        best_s, best_j = lax.top_k(cand_s.reshape(BLOCK, PEER_HEADS, -1), PEER_TOPK)
        eidx = jnp.take_along_axis(cand_i.reshape(BLOCK, PEER_HEADS, -1), best_j, axis=-1)
        g = jax.nn.softmax(best_s, axis=-1)
        ue = u[eidx]
        ve = v[eidx]
        act = jax.nn.gelu(jnp.einsum('thkd,td->thk', ue, xb).astype(jnp.float32), approximate=False)
        return jnp.einsum('thk,thkd->td', (g * act).astype(ve.dtype), ve)

    return lax.map(one_block, hb).reshape(Bn, S, D)

def setup_inputs(seed: int = 0) -> dict:
    key = jax.random.key(seed)
    ks = jax.random.split(key, 24)
    f32 = jnp.float32

    def nrm(k, shape, scale):
        return jax.random.normal(k, shape, f32) * scale

    def gain(k, n):
        return 1.0 + 0.02 * jax.random.normal(k, (n,), f32)

    return {
        'x': jax.random.normal(ks[0], (BATCH, SEQ, D_MODEL), f32),
        'positions': jnp.broadcast_to(jnp.arange(SEQ, dtype=jnp.int32), (BATCH, SEQ)),
        'norm_mix0': gain(ks[1], D_MODEL),
        'w_in0': nrm(ks[2], (D_MODEL, IN0_COLS), D_MODEL ** -0.5),
        'sinks0': nrm(ks[3], (A_Q_HEADS,), 0.5),
        'conv_w0': nrm(ks[4], (CONV_WIDTH, B_WIDTH), CONV_WIDTH ** -0.5),
        'w_out0': nrm(ks[5], (MIX0_WIDTH, D_MODEL), MIX0_WIDTH ** -0.5),
        'norm_ffn0': gain(ks[6], D_MODEL),
        'peer_wq0': nrm(ks[7], (D_MODEL, PEER_HEADS * PEER_QDIM), D_MODEL ** -0.5),
        'peer_keys0': nrm(ks[8], (PEER_HEADS, 2, PEER_N_KEYS, PEER_HALF), PEER_HALF ** -0.5),
        'peer_u0': nrm(ks[9], (PEER_EXPERTS, D_MODEL), D_MODEL ** -0.5),
        'peer_v0': nrm(ks[10], (PEER_EXPERTS, D_MODEL), 0.25),
        'norm_mix1': gain(ks[11], D_MODEL),
        'w_in1': nrm(ks[12], (D_MODEL, IN1_COLS), D_MODEL ** -0.5),
        'g_qa1': gain(ks[13], C_Q_RANK),
        'w_uq1': nrm(ks[14], (C_Q_RANK, UQ_COLS), C_Q_RANK ** -0.5),
        'w_out1': nrm(ks[15], (MIX1_WIDTH, D_MODEL), MIX1_WIDTH ** -0.5),
        'norm_ffn1': gain(ks[16], D_MODEL),
        'peer_wq1': nrm(ks[17], (D_MODEL, PEER_HEADS * PEER_QDIM), D_MODEL ** -0.5),
        'peer_keys1': nrm(ks[18], (PEER_HEADS, 2, PEER_N_KEYS, PEER_HALF), PEER_HALF ** -0.5),
        'peer_u1': nrm(ks[19], (PEER_EXPERTS, D_MODEL), D_MODEL ** -0.5),
        'peer_v1': nrm(ks[20], (PEER_EXPERTS, D_MODEL), 0.25),
        'norm_final': gain(ks[21], D_MODEL),
    }

def reference(x, positions,
              norm_mix0, w_in0, sinks0, conv_w0, w_out0,
              norm_ffn0, peer_wq0, peer_keys0, peer_u0, peer_v0,
              norm_mix1, w_in1, g_qa1, w_uq1, w_out1,
              norm_ffn1, peer_wq1, peer_keys1, peer_u1, peer_v1,
              norm_final):
    mixer_params = [(norm_mix0, w_in0, sinks0, conv_w0, w_out0),
                    (norm_mix1, w_in1, g_qa1, w_uq1, w_out1)]
    ffn_params = [(norm_ffn0, peer_wq0, peer_keys0, peer_u0, peer_v0),
                  (norm_ffn1, peer_wq1, peer_keys1, peer_u1, peer_v1)]
    for layer in range(DEPTH):
        if layer % 2 == 0:
            x = even_mixer(x, positions, *mixer_params[layer])
        else:
            x = odd_mixer(x, positions, *mixer_params[layer])
        g_ffn, wq, keys, u, v = ffn_params[layer]
        x = x + peer_ffn(rms_norm(x, g_ffn), wq, keys, u, v)
    return rms_norm(x, norm_final)


_drawn_inputs = setup_inputs


def setup_inputs(seed=0):
    import zlib

    import numpy as np

    out = dict(_drawn_inputs(seed))
    spreads = {}
    factors = {'sinks0': 3.546, 'g_qa1': 2.877, 'norm_ffn1': 3.737, 'norm_final': 2.76}
    for name, (base, spread) in spreads.items():
        noise = np.random.default_rng([zlib.crc32(name.encode()), seed]).standard_normal(out[name].shape)
        drawn = base * np.exp(spread * noise) if base else spread * noise
        out[name] = __import__('jax').numpy.asarray(drawn.astype(out[name].dtype))
    for name, factor in factors.items():
        out[name] = (out[name] * factor).astype(out[name].dtype)
    return out
```

```python
from contextlib import ExitStack

import numpy as np

import concourse.bass as bass
from concourse import mybir

P = 128
D = 2048
T = 256
NB = T // P
KT_ = D // P
CH = 512
EPS = 1e-5
NEG = -1e30
TAKEN = -3e38
ROPE_THETA = 500000.0
HALF_ROT = 16
CONV_COLS = 1024
Q_RANK = 512
IN1_COLS = 848
TOPK_KEYS = 64
HEADS = 16
PEER_H = 8
PEER_K = 16
NKEY = 128
SLOTS = PEER_H * PEER_K
RING = 8
WSLOTS = 4

TR_STAGES = [("h0", 8), ("qk0", 6), ("keys0", 4), ("h1", 8), ("h2", 8), ("cq", 2), ("qk1", 13),
             ("keys1", 4), ("h3", 8)]
PROJ = [("in0_qkv", 6, 3), ("in0_conv", 12, 6), ("out0", 8, 4), ("wq0", 8, 4), ("in1", 4, 2),
        ("uq", 3, 6), ("out1", 8, 4), ("wq1", 8, 4)]


HEAD_OF_PLACE = [(0, 2, 1, 3), (0, 1, 2, 3)]


def before(table, name, col=1):
    n = 0
    for row in table:
        if row[0] == name:
            return n
        n += row[col]
    return n


def program(nc, x, positions, norm_mix0, w_in0, sinks0, conv_w0, w_out0, norm_ffn0, peer_wq0,
            peer_keys0, peer_u0, peer_v0, norm_mix1, w_in1, g_qa1, w_uq1, w_out1, norm_ffn1,
            peer_wq1, peer_keys1, peer_u1, peer_v1, norm_final, out):
    fp32 = mybir.dt.float32
    u32 = mybir.dt.uint32
    i32 = mybir.dt.int32
    ALU = mybir.AluOpType
    ACT = mybir.ActivationFunctionType
    AX = mybir.AxisListType
    ctx = ExitStack()
    with ctx:
        def sb(name, shape, dt=fp32):
            return ctx.enter_context(nc.sbuf_tensor(name, shape, dt))

        def sem(name):
            return ctx.enter_context(nc.semaphore(name))

        X = sb("X", [P, NB, D])
        H = sb("H", [P, NB, D])
        HT = sb("HT", [P, KT_, T])
        MT = sb("MT", [P, KT_, T])
        PR = sb("PR", [P, 9216])
        A = sb("A", [P, 4096])
        ring = sb("ring", [P, RING, D])
        gain = sb("gain", [P, D])
        gain_q = sb("gain_q", [P, Q_RANK])
        kdup = sb("kdup", [P, 1024])
        KT = sb("KT", [P, 1024])
        ident = sb("ident", [P, P])
        band = sb("band", [P, T])
        keep = sb("keep", [P, NB, T])
        iota16 = sb("iota16", [P, PEER_K])
        sinks_in = sb("sinks_in", [P, HEADS])
        sinks = sb("sinks", [P, HEADS])
        conv_w = sb("conv_w", [P, 3, 8])
        pos_i = sb("pos_i", [P, NB], i32)
        pos_f = sb("pos_f", [P, NB])
        cosT = sb("cosT", [P, NB, HALF_ROT])
        sinT = sb("sinT", [P, NB, HALF_ROT])
        ang = sb("ang", [P, NB, HALF_ROT])
        turns = sb("turns", [P, NB, HALF_ROT])
        stat = sb("stat", [P, 8, NB])
        soft = sb("soft", [P, 2, 6, 4])
        iw = sb("iw", [P, NB, HEADS])
        score = sb("score", [P, T])
        max8 = sb("max8", [P, 8])
        gsum = sb("gsum", [P, 2, PEER_H])
        gate = sb("gate", [P, NB, SLOTS])
        eidx = sb("eidx", [P, NB, SLOTS], u32)
        cur = sb("cur", [P, 2, 8], u32)
        dots16 = sb("dots16", [P, PEER_K])
        dots = sb("dots", [P, SLOTS])
        gelu = sb("gelu", [P, SLOTS])
        wgt = sb("wgt", [P, SLOTS])
        ps = ctx.enter_context(nc.psum_tensor("ps", [P, 8 * 512], fp32))

        def flat(t):
            return t[:, :, :].rearrange("p a b -> p (a b)")

        Hf, MTf = flat(H), flat(MT)
        QKV = PR[:, 0:3072].rearrange("p (b n) -> p b n", b=NB)
        GATES = PR[:, 3072:9216].rearrange("p (g t) -> p g t", t=T)
        C1 = PR[:, 0:2 * IN1_COLS].rearrange("p (b n) -> p b n", b=NB)
        UQ = PR[:, 2 * IN1_COLS:2 * IN1_COLS + 6144].rearrange("p (b n) -> p b n", b=NB)
        PQT = PR[:, 0:4096].rearrange("p (g t) -> p g t", t=T)
        PKT = PR[:, 4096:6144].rearrange("p (g n) -> p g n", n=NKEY)
        PKN = PR[:, 6144:8192].rearrange("p (g n) -> p g n", n=NKEY)
        IQT = Hf[:, 2048:4096].rearrange("p (g t) -> p g t", t=T)
        rope_tmp = Hf[:, 0:2048].rearrange("p (k n) -> p k n", k=4)
        SC = A[:, 0:2048].rearrange("p (q h k) -> p q h k", q=2, h=4)
        PT = A[:, 2048:4096].rearrange("p (q h n) -> p q h n", q=2, h=4)
        IXL = A[:, :].rearrange("p (h k) -> p h k", h=HEADS)
        def inA(at, groups, n):
            return A[:, at:at + groups * n].rearrange("p (g n) -> p g n", n=n)

        top_s, top_i = inA(0, 2 * PEER_H, PEER_K), inA(256, 2 * PEER_H, PEER_K).bitcast(u32)
        best_s, best_j = inA(512, PEER_H, PEER_K), inA(640, PEER_H, PEER_K).bitcast(u32)
        half_j, half_i = inA(768, 2, SLOTS).bitcast(u32), inA(1024, 2, SLOTS)
        wring = ring[:, :, :].rearrange("p (s two) n -> p s (two n)", two=2)

        def wtile(slot, width=CH):
            return wring[:, slot, :].rearrange("p (k n) -> p k n", n=width)

        def bank(i, n=1, w=512):
            return ps[:, i * 512:(i + n - 1) * 512 + w]

        x_loaded, gain_loaded, small_loaded = sem("x_loaded"), sem("gain_loaded"), sem("small_loaded")
        keys_loaded, out_stored = sem("keys_loaded"), sem("out_stored")
        w_loaded = [sem(f"w_loaded{i}") for i in range(WSLOTS)]
        w_used = sem("w_used")
        consts_ready = sem("consts_ready")
        conv_done = sem("conv_done")
        angles_ready, sines_ready = sem("angles_ready"), sem("sines_ready")
        sq_done, var_ready, root_ready, h_ready = (sem("sq_done"), sem("var_ready"),
                                                   sem("root_ready"), sem("h_ready"))
        cq_sq, cq_var, cq_root, cq_ready = sem("cq_sq"), sem("cq_var"), sem("cq_root"), sem("cq_ready")
        tr_done, tr_copied = sem("tr_done"), sem("tr_copied")
        chunk_done, chunk_copied, chunk_added = sem("chunk_done"), sem("chunk_copied"), sem("chunk_added")
        roped = sem("roped")
        ix_done, ix_read = sem("ix_done"), sem("ix_read")
        sc_done, sc_read, exp_done, prob_ready = (sem("sc_done"), sem("sc_read"), sem("exp_done"),
                                                  sem("prob_ready"))
        pt_done, pt_copied, pv_done, pv_copied = (sem("pt_done"), sem("pt_copied"), sem("pv_done"),
                                                  sem("pv_copied"))
        rs_done, best_ready, gexp_done, routed = (sem("rs_done"), sem("best_ready"),
                                                  sem("gexp_done"), sem("routed"))
        idx_cur = sem("idx_cur")
        landed = [sem(f"landed{i}") for i in range(RING)]
        ring_free = sem("ring_free")
        dots_saved, dots_ready, gelu_ready = sem("dots_saved"), sem("dots_ready"), sem("gelu_ready")
        vec_step, act_step, pool_step = sem("vec_step"), sem("act_step"), sem("pool_step")

        gains = [norm_mix0, norm_ffn0, norm_mix1, norm_ffn1, norm_final]
        keys_dram = [peer_keys0, peer_keys1]
        u_dram, v_dram = [peer_u0, peer_u1], [peer_v0, peer_v1]
        TILES = sum(p[1] for p in PROJ)

        def transposes(stage):
            def pack(srcs, dst):
                return [(srcs[i:i + 4], dst(i)) for i in range(0, len(srcs), 4)]
            if stage in ("h0", "h1", "h2", "h3"):
                return [e for b in range(NB) for e in pack(
                    [H[:, b, k * P:(k + 1) * P] for k in range(KT_)],
                    lambda i, b=b: HT[:, i:i + 4, b * P:(b + 1) * P])]
            if stage in ("keys0", "keys1"):
                return pack([PKN[:, g, :] for g in range(2 * PEER_H)], lambda i: PKT[:, i:i + 4, :])
            if stage == "cq":
                return [e for b in range(NB) for e in pack(
                    [C1[:, b, k * P:(k + 1) * P] for k in range(Q_RANK // P)],
                    lambda i, b=b: MT[:, i:i + 4, b * P:(b + 1) * P])]
            if stage == "qk0":
                kd = kdup[:, :].rearrange("p (b g n) -> p b g n", b=NB, g=4)
                kt = KT[:, :].rearrange("p (g t) -> p g t", g=4)
                return [e for b in range(NB) for e in
                        pack([QKV[:, b, k * P:(k + 1) * P] for k in range(8)],
                             lambda i, b=b: HT[:, i:i + 4, b * P:(b + 1) * P])
                        + pack([kd[:, b, g, :] for g in range(4)],
                               lambda i, b=b: kt[:, :, b * P:(b + 1) * P])]
            return ([e for b in range(NB) for e in
                     pack([UQ[:, b, h * P:(h + 1) * P] for h in range(HEADS)],
                          lambda i, b=b: HT[:, i:i + 4, b * P:(b + 1) * P])
                     + pack([UQ[:, b, 2048 + t * P:2048 + (t + 1) * P] for t in range(8)],
                            lambda i, b=b: IQT[:, i:i + 4, b * P:(b + 1) * P])]
                    + pack([C1[:, b, 512:640] for b in range(NB)]
                           + [kdup[:, b * P:(b + 1) * P] for b in range(NB)],
                           lambda i: KT[:, 0:512].rearrange("p (g n) -> p g n", g=4)))

        block = ctx.enter_context(nc.Block())

        @block.sync
        def _(sp):
            for b in range(NB):
                sp.dma_start(X[:, b, :], x[0, b * P:(b + 1) * P, :]).then_inc(x_loaded, 16)
            sp.dma_start(gain[:, :], gains[0].partition_broadcast(P)).then_inc(small_loaded, 16)
            with nc.allow_non_contiguous_dma(reason="a few small vectors laid over the partitions"):
                sp.dma_start(pos_i[:, :], positions.rearrange("o (b p) -> p (o b)", p=P)).then_inc(small_loaded, 16)
            sp.dma_start(sinks_in[:, :], sinks0.partition_broadcast(P)).then_inc(small_loaded, 16)
            with nc.allow_non_contiguous_dma(reason="a few small vectors laid over the partitions"):
                sp.dma_start(conv_w[:, :, :], conv_w0.rearrange("w (c p) -> p w c", p=P)).then_inc(small_loaded, 16)
            sp.dma_start(gain_q[:, :], g_qa1.partition_broadcast(P)).then_inc(small_loaded, 16)

            def load_tile(n, src, slot, waits=True, width=CH):
                if waits:
                    sp.wait_ge(w_used, n - WSLOTS + 1)
                sp.dma_start(wtile(slot, width), src).then_inc(w_loaded[slot], 16)

            def load_chunks(name, w, c0, chunks):
                w = w.rearrange("(h k p) n -> h p k n", h=2, p=P)
                n0 = before(PROJ, name)
                with sp.Fori(0, chunks // 2) as i:
                    for c in range(2):
                        for h in range(2):
                            s = 2 * c + h
                            load_tile(i * 4 + (n0 + s), w[h][:, :, bass.ds((i * 2 + (c0 + c)) * CH, CH)],
                                      (n0 + s) % WSLOTS)

            w = w_in0.rearrange("(h k p) n -> h p k n", h=2, p=P)
            for n in range(6):
                load_tile(n, w[n % 2][:, :, (n // 2) * CH:(n // 2 + 1) * CH], n % WSLOTS, waits=n >= WSLOTS)
            load_chunks("in0_conv", w_in0, 3, 6)
            load_chunks("out0", w_out0, 0, 4)
            load_chunks("wq0", peer_wq0, 0, 4)
            sp.wait_ge(ring_free, RING + 4 * SLOTS)
            w = w_in1.rearrange("(h k p) n -> h p k n", h=2, p=P)
            n0 = before(PROJ, "in1")
            for n in range(4):
                c, width = n // 2, (CH, IN1_COLS - CH)[n // 2]
                sp.wait_ge(w_used, n0 + n - WSLOTS + 1)
                sp.dma_start(wtile((n0 + n) % WSLOTS)[:, :, 0:width],
                             w[n % 2][:, :, c * CH:c * CH + width]).then_inc(w_loaded[(n0 + n) % WSLOTS], 16)
            n0 = before(PROJ, "uq")
            w = w_uq1.rearrange("(k p) n -> p k n", p=P)
            for n in range(3):
                load_tile(n0 + n, w[:, :, n * 1024:(n + 1) * 1024], (n0 + n) % WSLOTS, width=1024)
            load_chunks("out1", w_out1, 0, 4)
            load_chunks("wq1", peer_wq1, 0, 4)
            sp.wait_ge(h_ready, 10)
            for b in range(NB):
                sp.dma_start(out[0, b * P:(b + 1) * P, :], H[:, b, :]).then_inc(out_stored, 16)
            sp.wait_ge(out_stored, 16 * NB)

        @block.gpsimd
        def _(pool):
            steps = [0]

            def link(ins):
                steps[0] += 1
                ins.then_inc(pool_step, 1)
                pool.wait_ge(pool_step, steps[0])

            nc.gpsimd.iota(iota16[:, :], pattern=[[1, PEER_K]], base=0, channel_multiplier=0,
                           allow_small_or_imprecise_dtypes=True)
            nc.gpsimd.memset(ident[:, :], 0.0)
            link(nc.gpsimd.memset(band[:, :], 0.0))
            nc.gpsimd.affine_select(out=ident[:, :], in_=ident[:, :], compare_op=ALU.not_equal, fill=1.0,
                                    base=0, pattern=[[-1, P]], channel_multiplier=1)
            nc.gpsimd.affine_select(out=band[:, 0:P], in_=band[:, 0:P], compare_op=ALU.is_gt, fill=NEG,
                                    base=0, pattern=[[1, P]], channel_multiplier=-1)
            nc.gpsimd.affine_select(out=band[:, P:T], in_=band[:, P:T], compare_op=ALU.is_ge, fill=NEG,
                                    base=0, pattern=[[-1, P]], channel_multiplier=1).then_inc(consts_ready, 1)

            def load_gain(n):
                pool.wait_ge(h_ready, 2 * n)
                pool.dma_start(gain[:, :], gains[n].partition_broadcast(P)).then_inc(gain_loaded, 16)

            load_gain(1)
            bg, cg, hx = (GATES[:, 8 * i:8 * i + 8, :] for i in range(3))
            tmp = MT[:, 8:16, :]

            def tap(w):
                return conv_w[:, w, :].unsqueeze(2).broadcast_to([P, 8, T])

            pool.wait_ge(small_loaded, 80)
            pool.wait_ge(chunk_copied, 9)
            link(nc.gpsimd.tensor_tensor(cg, cg, hx, ALU.mult))
            nc.gpsimd.tensor_tensor(hx, cg, tap(2), ALU.mult)
            link(nc.gpsimd.tensor_tensor(tmp, cg, tap(1), ALU.mult))
            link(nc.gpsimd.tensor_tensor(hx[:, :, 1:T], hx[:, :, 1:T], tmp[:, :, 0:T - 1], ALU.add))
            link(nc.gpsimd.tensor_tensor(tmp, cg, tap(0), ALU.mult))
            link(nc.gpsimd.tensor_tensor(hx[:, :, 2:T], hx[:, :, 2:T], tmp[:, :, 0:T - 2], ALU.add))
            nc.gpsimd.tensor_tensor(tmp, hx, bg, ALU.mult).then_inc(conv_done, 1)

            def load_keys(layer):
                pool.wait_ge(pv_done, 8 * (layer + 1))
                if layer == 0:
                    pool.wait_ge(conv_done, 1)
                pool.dma_start(PKN, keys_dram[layer].rearrange("h c n d -> n (h c) d")).then_inc(keys_loaded, 16)

            def gather(layer, b, table, phase):
                with pool.Fori(0, PEER_H) as i:
                    for o in range(2):
                        nc.gpsimd.tensor_copy(cur[:, o, :], eidx[:, b, bass.ds(i * 16 + o * 8, 8)]).then_inc(idx_cur, 1)
                        pool.wait_ge(idx_cur, i * 2 + (phase * 16 + o + 1))
                        pool.nop(nofuse=True)
                        for r in range(RING):
                            pool.wait_ge(ring_free, i * 16 + (phase * SLOTS + o * 8 + r + 1))
                            pool.nop(nofuse=True)
                            pool.indirect_dma_start(ring[:, r, :], None, table,
                                                    bass.IndirectOffsetOnAxis(cur[:, o, r:r + 1], 0)).then_inc(landed[r], 16)

            def gathers(layer):
                pool.wait_ge(w_used, before(PROJ, f"wq{layer}") + 8)
                for b in range(NB):
                    pool.wait_ge(routed, layer * NB + b + 1)
                    gather(layer, b, u_dram[layer], layer * 4 + b * 2)
                    gather(layer, b, v_dram[layer], layer * 4 + b * 2 + 1)

            load_keys(0)
            load_gain(2)
            gathers(0)
            load_gain(3)
            load_keys(1)
            load_gain(4)
            gathers(1)

        @block.scalar
        def _(act):
            steps = [0]

            def link(ins):
                steps[0] += 1
                ins.then_inc(act_step, 1)
                act.wait_ge(act_step, steps[0])

            act.wait_ge(angles_ready, 1)
            nc.scalar.activation(sinT[:, :, :], ang[:, :, :], ACT.Sin)
            nc.scalar.activation(cosT[:, :, :], ang[:, :, :], ACT.Sin, scale=0.5).then_inc(sines_ready, 1)

            def squares(n):
                for b in range(NB):
                    nc.scalar.activation(H[:, b, :], X[:, b, :], ACT.Square,
                                         accum_out=stat[:, 0, b:b + 1]).then_inc(sq_done, 1)
                act.wait_ge(var_ready, n + 1)
                nc.scalar.activation(stat[:, 3, :], stat[:, 2, :], ACT.Sqrt).then_inc(root_ready, 1)

            def copy_transposes(stage):
                n0 = before(TR_STAGES, stage)
                for n, (srcs, dst) in enumerate(transposes(stage)):
                    act.wait_ge(tr_done, n0 + n + 1)
                    nc.scalar.copy(dst, bank(n % 8).rearrange("p (g n) -> p g n", n=P)).then_inc(tr_copied, 1)

            def copy_channels(name, dst, chunks):
                m0 = before(PROJ, name, 2)
                with act.Fori(0, chunks // 2) as i:
                    for c in range(2):
                        act.wait_ge(chunk_done, i * 2 + (m0 + c + 1))
                        src = bank(4 * ((m0 + c) % 2), 4).rearrange("p (g n) -> p g n", n=512)[:, :, 0:T]
                        nc.scalar.copy(dst[:, bass.ds(i * 8 + c * 4, 4), :], src).then_inc(chunk_copied, 1)

            def copied_before(name):
                return sum(p[2] for p in PROJ[:[q[0] for q in PROJ].index(name)] if not p[0].startswith("out"))

            def copy_tokens(m, dst, width=CH):
                act.wait_ge(chunk_done, m + 1)
                for b in range(NB):
                    last = nc.scalar.copy(dst[:, b, :], bank(4 * (m % 2) + b, w=width))
                last.then_inc(chunk_copied, 1)

            def attention(layer):
                def exps(q):
                    act.wait_ge(sc_read, q + 1)
                    pr, nk = q % 2, (q % 8) // 4 + 1
                    for h in range(4):
                        last = nc.scalar.activation(SC[:, pr, h, 0:nk * P], SC[:, pr, h, 0:nk * P], ACT.Exp,
                                                    bias=soft[:, pr, 0, h:h + 1], accum_out=soft[:, pr, 1, h:h + 1])
                    if layer == 0:
                        last = nc.scalar.activation(soft[:, pr, 3, :], soft[:, pr, 2, :], ACT.Exp)
                    last.then_inc(exp_done, 1)

                def copy_out(q):
                    pr, b, g, nk = q % 2, (q % 8) // 4, q % 4, (q % 8) // 4 + 1
                    act.wait_ge(pt_done, q + 1)
                    if q >= 2:
                        act.wait_ge(pv_done, q - 1)
                    src = bank(4, 2).rearrange("p (h n) -> p h n", h=4)[:, :, 0:nk * P]
                    nc.scalar.copy(PT[:, pr, :, 0:nk * P], src).then_inc(pt_copied, 1)
                    act.wait_ge(pv_done, q + 1)
                    n = (2, 4)[layer]
                    nc.scalar.copy(MT[:, n * g:n * g + n, b * P:(b + 1) * P],
                                   bank(6 + pr, w=n * P).rearrange("p (h n) -> p h n", h=n)).then_inc(pv_copied, 1)

                q0 = layer * 8
                exps(q0)
                for q in range(q0, q0 + 8):
                    if q + 1 < q0 + 8:
                        exps(q + 1)
                    copy_out(q)

            def peer(layer):
                copy_transposes(f"keys{layer}")
                act.wait_ge(chunk_added, 2 + 4 * (layer + 1))
                squares(2 * layer + 1)
                copy_transposes(f"h{2 * layer + 1}")
                copy_channels(f"wq{layer}", PQT, 4)
                for b in range(NB):
                    act.wait_ge(best_ready, layer * NB + b + 1)
                    nc.scalar.activation(gate[:, b, :], gate[:, b, :], ACT.Exp).then_inc(gexp_done, 1)
                for b in range(NB):
                    act.wait_ge(dots_ready, layer * NB + b + 1)
                    nc.scalar.activation(gelu[:, :], dots[:, :], ACT.Gelu).then_inc(gelu_ready, 1)
                act.wait_ge(ring_free, RING + 4 * SLOTS * (layer + 1))
                squares(2 * layer + 2)

            act.wait_ge(x_loaded, 32)
            squares(0)
            copy_transposes("h0")
            for c in range(3):
                copy_tokens(c, QKV[:, :, c * CH:(c + 1) * CH])
            copy_channels("in0_conv", GATES, 6)
            copy_transposes("qk0")
            attention(0)
            peer(0)
            copy_transposes("h2")
            m0 = before(PROJ, "in1", 2)
            copy_tokens(m0, C1[:, :, 0:CH])
            copy_tokens(m0 + 1, C1[:, :, CH:IN1_COLS], IN1_COLS - CH)
            act.wait_ge(chunk_copied, copied_before("uq"))
            for b in range(NB):
                nc.scalar.activation(A[:, b * CH:(b + 1) * CH], C1[:, b, 0:CH], ACT.Square,
                                     accum_out=stat[:, 0, b:b + 1]).then_inc(cq_sq, 1)
            act.wait_ge(cq_var, 1)
            nc.scalar.activation(stat[:, 3, :], stat[:, 2, :], ACT.Sqrt).then_inc(cq_root, 1)
            copy_transposes("cq")
            m0 = before(PROJ, "uq", 2)
            for c in range(6):
                copy_tokens(m0 + c, UQ[:, :, c * CH:(c + 1) * CH])
            copy_transposes("qk1")
            attention(1)
            peer(1)

        @block.tensor
        def _(pe):
            def transpose_stage(stage):
                n0 = before(TR_STAGES, stage)
                for n, (srcs, dst) in enumerate(transposes(stage)):
                    if n >= 8:
                        pe.wait_ge(tr_copied, n0 + n - 7)
                    for i, s in enumerate(srcs):
                        last = nc.tensor.transpose(ps[:, (n % 8) * 512 + i * P:(n % 8) * 512 + (i + 1) * P],
                                                   s, ident[:, :])
                    last.then_inc(tr_done, 1)

            def transposed(stage):
                pe.wait_ge(tr_copied, before(TR_STAGES, stage) + dict(TR_STAGES)[stage])

            def token_chunk(m, tiles, lhs, width=CH, kper=8, col=0, freed=True):
                last = None
                for t, (n, slot, count) in enumerate(tiles):
                    pe.wait_ge(w_loaded[slot], count)
                    for k in range(kper):
                        kk = t * kper + k
                        for b in range(NB):
                            last = nc.tensor.matmul(bank(4 * (m % 2) + b, w=width), lhs[:, kk, b * P:(b + 1) * P],
                                                    wtile(slot, 1024 if kper == 4 else CH)[:, k, col:col + width],
                                                    start=(kk == 0), stop=(kk == len(tiles) * kper - 1))
                    if freed and t < len(tiles) - 1:
                        last.then_inc(w_used, 1)
                return last

            def tile_at(n):
                return n, n % WSLOTS, 16 * (n // WSLOTS + 1)

            def chunk_loop(name, chunks, lhs, channels, drained):
                n0, m0 = before(PROJ, name), before(PROJ, name, 2)
                d0 = sum(p[2] for p in PROJ[:[q[0] for q in PROJ].index(name)]
                         if p[0].startswith("out") == (drained is chunk_added)) + 2 * (drained is chunk_added)
                with pe.Fori(0, chunks // 2) as i:
                    for c in range(2):
                        pe.wait_ge(drained, i * 2 + (d0 + c - 1))
                        for t in range(2):
                            n = n0 + 2 * c + t
                            pe.wait_ge(w_loaded[n % WSLOTS], i * 16 + 16 * (n // WSLOTS + 1))
                            for k in range(8):
                                kk = 8 * t + k
                                if channels:
                                    for g in range(4):
                                        last = nc.tensor.matmul(bank(4 * ((m0 + c) % 2) + g, w=T),
                                                                wtile(n % WSLOTS)[:, k, g * P:(g + 1) * P],
                                                                lhs[:, kk, :], start=(kk == 0), stop=(kk == 15))
                                else:
                                    for b in range(NB):
                                        last = nc.tensor.matmul(bank(4 * ((m0 + c) % 2) + b),
                                                                lhs[:, kk, b * P:(b + 1) * P],
                                                                wtile(n % WSLOTS)[:, k, :],
                                                                start=(kk == 0), stop=(kk == 15))
                            last.then_inc(w_used, 1)
                        pe.wait_ge(w_used, i * 4 + (n0 + 2 * c + 2))
                        pe.nop(nofuse=True).then_inc(chunk_done, 1)

            def token_chunks(name, chunks, lhs, widths):
                n0, m0 = before(PROJ, name), before(PROJ, name, 2)
                d0 = sum(p[2] for p in PROJ[:[q[0] for q in PROJ].index(name)] if not p[0].startswith("out"))
                for c in range(chunks):
                    if c >= 2:
                        pe.wait_ge(chunk_copied, d0 + c - 1)
                    last = token_chunk(m0 + c, [tile_at(n0 + 2 * c), tile_at(n0 + 2 * c + 1)], lhs, widths[c])
                    last.then_inc(w_used, 1)
                    pe.wait_ge(w_used, n0 + 2 * c + 2)
                    pe.nop(nofuse=True).then_inc(chunk_done, 1)

            def attention(layer):
                scale_rows = (64, P)[layer]

                def scores(q):
                    pr, b, g, nk = q % 2, (q % 8) // 4, q % 4, (q % 8) // 4 + 1
                    if q % 8 >= 2:
                        pe.wait_ge(sc_read, q - 1)
                    if layer == 1:
                        pe.wait_ge(ix_read, 8)
                    for i in range(4):
                        h = 4 * g + HEAD_OF_PLACE[layer][i]
                        o = ps[:, pr * 1024 + i * T:pr * 1024 + i * T + nk * P]
                        if layer == 0:
                            r = 64 * (h % 2)
                            lhs = HT[r:r + 64, h // 2, b * P:(b + 1) * P]
                            rhs = KT[r:r + 64, g * T:g * T + nk * P]
                        else:
                            lhs, rhs = HT[:, h, b * P:(b + 1) * P], KT[:, 0:nk * P]
                        last = nc.tensor.matmul(o, lhs, rhs, start=True, stop=True)
                    last.then_inc(sc_done, 1)

                def values(q):
                    pr, b, g, nk = q % 2, (q % 8) // 4, q % 4, (q % 8) // 4 + 1
                    pe.wait_ge(prob_ready, q + 1)
                    if q >= 1:
                        pe.wait_ge(pt_copied, q)
                    for i in range(4):
                        for kb in range(nk):
                            last = nc.tensor.transpose(ps[:, 2048 + i * T + kb * P:2048 + i * T + (kb + 1) * P],
                                                       SC[:, pr, i, kb * P:(kb + 1) * P], ident[:, :])
                    last.then_inc(pt_done, 1)
                    pe.wait_ge(pt_copied, q + 1)
                    if q >= 2:
                        pe.wait_ge(pv_copied, q - 1)
                    for i in range(4):
                        h = 4 * g + HEAD_OF_PLACE[layer][i]
                        for kb in range(nk):
                            if layer == 0:
                                r = 64 * (h % 2)
                                c = (6 + pr) * 512 + (h % 4 // 2) * P
                                o = ps[r:r + 64, c:c + P]
                                lhs = QKV[:, kb, 1280 + g * 64:1280 + (g + 1) * 64]
                            else:
                                o = ps[:, (6 + pr) * 512 + i * P:(6 + pr) * 512 + (i + 1) * P]
                                lhs = C1[:, kb, 640:768]
                            last = nc.tensor.matmul(o, lhs, PT[:, pr, i, kb * P:(kb + 1) * P],
                                                    start=(kb == 0), stop=(kb == nk - 1))
                    last.then_inc(pv_done, 1)

                q0 = layer * 8
                scores(q0)
                for q in range(q0, q0 + 8):
                    if q + 1 < q0 + 8:
                        scores(q + 1)
                    values(q)

            def peer(layer):
                pe.wait_ge(keys_loaded, 16 * (layer + 1))
                pe.wait_ge(chunk_added, 2 + 4 * (layer + 1))
                transpose_stage(f"keys{layer}")
                transposed(f"keys{layer}")
                pe.wait_ge(h_ready, 4 * layer + 4)
                transpose_stage(f"h{2 * layer + 1}")
                transposed(f"h{2 * layer + 1}")
                chunk_loop(f"wq{layer}", 4, HT, True, chunk_copied)
                pe.wait_ge(chunk_copied, (13, 25)[layer])
                for b in range(NB):
                    for g in range(2 * PEER_H):
                        last = nc.tensor.matmul(ps[:, b * 2048 + g * NKEY:b * 2048 + (g + 1) * NKEY],
                                                PQT[:, g, b * P:(b + 1) * P], PKT[:, g, :], start=True, stop=True)
                    last.then_inc(rs_done, 1)
                pe.wait_ge(routed, 2 * (layer + 1))

            pe.wait_ge(consts_ready, 1)
            pe.wait_ge(h_ready, 2)
            transpose_stage("h0")
            transposed("h0")
            token_chunks("in0_qkv", 3, HT, [CH] * 3)
            pe.wait_ge(chunk_copied, 3)
            chunk_loop("in0_conv", 6, HT, True, chunk_copied)
            pe.wait_ge(chunk_copied, 9)
            pe.wait_ge(roped, 1)
            transpose_stage("qk0")
            transposed("qk0")
            attention(0)
            pe.wait_ge(pv_copied, 8)
            pe.wait_ge(conv_done, 1)
            chunk_loop("out0", 4, MT, False, chunk_added)
            peer(0)
            pe.wait_ge(h_ready, 6)
            transpose_stage("h2")
            transposed("h2")
            token_chunks("in1", 2, HT, [CH, IN1_COLS - CH])
            pe.wait_ge(cq_ready, 1)
            pe.wait_ge(chunk_copied, 15)
            transpose_stage("cq")
            transposed("cq")
            n0, m0 = before(PROJ, "uq"), before(PROJ, "uq", 2)
            for c in range(6):
                if c >= 2:
                    pe.wait_ge(chunk_copied, 15 + c - 1)
                tile = tile_at(n0 + c // 2)
                last = token_chunk(m0 + c, [tile], MT, kper=4, col=(c % 2) * CH, freed=False)
                if c % 2:
                    last.then_inc(w_used, 1)
                    pe.wait_ge(w_used, n0 + c // 2 + 1)
                    pe.nop(nofuse=True).then_inc(chunk_done, 1)
                else:
                    last.then_inc(chunk_done, 1)
            pe.wait_ge(chunk_copied, 21)
            pe.wait_ge(roped, 2)
            transpose_stage("qk1")
            transposed("qk1")
            for j in range(8):
                b, g, nk = j // 4, j % 4, j // 4 + 1
                if j >= 2:
                    pe.wait_ge(ix_read, j - 1)
                for i in range(4):
                    h = 4 * g + HEAD_OF_PLACE[0][i]
                    r = 64 * (h % 2)
                    last = nc.tensor.matmul(ps[:, (j % 2) * 1024 + i * T:(j % 2) * 1024 + i * T + nk * P],
                                            IQT[r:r + 64, h // 2, b * P:(b + 1) * P],
                                            KT[r:r + 64, T:T + nk * P], start=True, stop=True)
                last.then_inc(ix_done, 1)
            attention(1)
            pe.wait_ge(pv_copied, 16)
            chunk_loop("out1", 4, MT, False, chunk_added)
            peer(1)

        @block.vector
        def _(dve):
            steps = [0]
            V = nc.vector

            def link(ins):
                steps[0] += 1
                ins.then_inc(vec_step, 1)
                dve.wait_ge(vec_step, steps[0])

            V.memset(max8[:, :], 0.0).then_inc(ring_free, RING)
            V.memset(wgt[:, :], 0.0).then_inc(chunk_added, 2)

            dve.wait_ge(small_loaded, 80)
            link(V.tensor_copy(pos_f[:, :], pos_i[:, :]))
            V.tensor_copy(sinks[:, :].rearrange("p (g o e) -> p g o e", o=2, e=2),
                          sinks_in[:, :].rearrange("p (g e o) -> p g o e", o=2, e=2))
            for i in range(HALF_ROT):
                inv = float(np.float32(ROPE_THETA) ** np.float32(-i * 2.0 / (2 * HALF_ROT)))
                last = V.tensor_scalar(ang[:, :, i], pos_f[:, :], inv, None, ALU.mult)
            link(last)
            magic = 1.5 * 2.0 ** 23
            c1 = 6.28125
            c2 = round((2 * np.pi - c1) * 2.0 ** 20) / 2.0 ** 20
            c3 = float(np.float32(2 * np.pi - c1 - c2))
            link(V.tensor_scalar(turns[:, :, :], ang[:, :, :], float(1 / (2 * np.pi)), magic, ALU.mult, ALU.add))
            link(V.tensor_scalar(turns[:, :, :], turns[:, :, :], magic, None, ALU.subtract))
            for c in (c1, c2, c3):
                link(V.scalar_tensor_tensor(out=ang[:, :, :], in0=turns[:, :, :], scalar=-c, in1=ang[:, :, :],
                                            op0=ALU.mult, op1=ALU.add))
            V.tensor_scalar(ang[:, :, :], ang[:, :, :], 3.1415925, -3.1415925, ALU.min, ALU.max).then_inc(angles_ready, 1)
            dve.wait_ge(sines_ready, 1)
            link(V.tensor_tensor(cosT[:, :, :], cosT[:, :, :], cosT[:, :, :], ALU.mult))
            link(V.tensor_scalar(cosT[:, :, :], cosT[:, :, :], -2.0, 1.0, ALU.mult, ALU.add))

            def inverse_root(width, summed, n_sum, var, root, n):
                dve.wait_ge(summed, n_sum)
                link(V.tensor_scalar(stat[:, 1, :], stat[:, 0, :], 1.0 / width, EPS, ALU.mult, ALU.add))
                V.reciprocal(stat[:, 2, :], stat[:, 1, :]).then_inc(var, 1)
                dve.wait_ge(root, n)
                link(V.tensor_tensor(stat[:, 4, :], stat[:, 3, :], stat[:, 3, :], ALU.mult))
                link(V.tensor_tensor(stat[:, 4, :], stat[:, 4, :], stat[:, 1, :], ALU.mult))
                link(V.tensor_scalar(stat[:, 4, :], stat[:, 4, :], -0.5, 1.5, ALU.mult, ALU.add))
                link(V.tensor_tensor(stat[:, 5, :], stat[:, 3, :], stat[:, 4, :], ALU.mult))

            def norm(n):
                inverse_root(D, sq_done, 2 * n + 2, var_ready, root_ready, n + 1)
                if n:
                    dve.wait_ge(gain_loaded, 16 * n)
                for b in range(NB):
                    V.scalar_tensor_tensor(out=H[:, b, :], in0=X[:, b, :], scalar=stat[:, 5, b:b + 1],
                                           in1=gain[:, :], op0=ALU.mult, op1=ALU.mult).then_inc(h_ready, 1)
                dve.wait_ge(h_ready, 2 * n + 2)

            def rope(x_, heads, dim):
                half = dim // 8
                v = x_.rearrange("p b (h d) -> p b h d", d=dim)
                a, b_ = v[:, :, :, 0:half], v[:, :, :, half:2 * half]
                step = HALF_ROT // half
                shape = [P, NB, heads, half]
                cs = cosT[:, :, 0:HALF_ROT:step].unsqueeze(2).broadcast_to(shape)
                sn = sinT[:, :, 0:HALF_ROT:step].unsqueeze(2).broadcast_to(shape)
                t = [rope_tmp[:, i, 0:NB * heads * half].rearrange("p (b h d) -> p b h d", b=NB, h=heads)
                     for i in range(4)]
                V.tensor_tensor(t[0], a, cs, ALU.mult)
                V.tensor_tensor(t[1], b_, sn, ALU.mult)
                V.tensor_tensor(t[2], b_, cs, ALU.mult)
                link(V.tensor_tensor(t[3], a, sn, ALU.mult))
                V.tensor_tensor(a, t[0], t[1], ALU.subtract)
                return V.tensor_tensor(b_, t[2], t[3], ALU.add)

            def attention(layer):
                scale = float((64, P)[layer]) ** -0.5

                def mask_scores(q):
                    pr, b, g, nk = q % 2, (q % 8) // 4, q % 4, (q % 8) // 4 + 1
                    dve.wait_ge(sc_done, q + 1)
                    if q >= 2:
                        dve.wait_ge(pt_done, q - 1)
                        dve.wait_ge(prob_ready, q - 1)
                    src = ps[:, pr * 1024:(pr + 1) * 1024].rearrange("p (h k) -> p h k", h=4)[:, :, 0:nk * P]
                    mask = (band[:, T - nk * P:T], keep[:, b, 0:nk * P])[layer]
                    s = SC[:, pr, :, 0:nk * P]
                    link(V.scalar_tensor_tensor(out=s, in0=src, scalar=scale,
                                                in1=mask.unsqueeze(1).broadcast_to([P, 4, nk * P]),
                                                op0=ALU.mult, op1=ALU.add))
                    link(V.reduce_max(soft[:, pr, 4, :], s, AX.X))
                    if layer == 0:
                        hs = sinks[:, 4 * g:4 * g + 4]
                        link(V.tensor_tensor(soft[:, pr, 4, :], soft[:, pr, 4, :], hs, ALU.max))
                        V.tensor_tensor(soft[:, pr, 2, :], hs, soft[:, pr, 4, :], ALU.subtract)
                    V.tensor_scalar(soft[:, pr, 0, :], soft[:, pr, 4, :], -1.0, None, ALU.mult).then_inc(sc_read, 1)

                def normalise(q):
                    pr, nk = q % 2, (q % 8) // 4 + 1
                    dve.wait_ge(exp_done, q + 1)
                    den = soft[:, pr, 1, :]
                    if layer == 0:
                        link(V.tensor_tensor(den, den, soft[:, pr, 3, :], ALU.add))
                    link(V.reciprocal(soft[:, pr, 5, :], den))
                    s = SC[:, pr, :, 0:nk * P]
                    V.tensor_tensor(s, s, soft[:, pr, 5, :].unsqueeze(2).broadcast_to([P, 4, nk * P]),
                                    ALU.mult).then_inc(prob_ready, 1)

                q0 = layer * 8
                mask_scores(q0)
                for q in range(q0, q0 + 8):
                    if q + 1 < q0 + 8:
                        mask_scores(q + 1)
                    normalise(q)
                dve.wait_ge(prob_ready, q0 + 8)

            def add_chunks(name, layer):
                m0 = before(PROJ, name, 2)
                with dve.Fori(0, 2) as i:
                    for c in range(2):
                        dve.wait_ge(chunk_done, i * 2 + (m0 + c + 1))
                        for b in range(NB):
                            cols = X[:, b, bass.ds(i * 1024 + c * CH, CH)]
                            last = V.tensor_tensor(cols, bank(4 * ((m0 + c) % 2) + b), cols, ALU.add)
                        last.then_inc(chunk_added, 1)
                dve.wait_ge(chunk_added, 2 + 4 * (layer + 1))

            def route(layer, b):
                dve.wait_ge(rs_done, layer * NB + b + 1)
                s = ps[:, b * 2048:(b + 1) * 2048].rearrange("p (g n) -> p g n", n=NKEY)
                rest = MTf[:, 0:2048].rearrange("p (g n) -> p g n", n=NKEY)
                G = 2 * PEER_H

                def top16(groups, vals, idxs, src, left):
                    for g in range(groups):
                        last = V.max(vals[:, g, 0:8], src[:, g, :])
                    link(last)
                    for g in range(groups):
                        V.max_index(idxs[:, g, 0:8], vals[:, g, 0:8], src[:, g, :])
                        last = V.match_replace(left[:, g, :], vals[:, g, 0:8], src[:, g, :], TAKEN)
                    link(last)
                    for g in range(groups):
                        last = V.max(vals[:, g, 8:16], left[:, g, :])
                    link(last)
                    for g in range(groups):
                        last = V.max_index(idxs[:, g, 8:16], vals[:, g, 8:16], left[:, g, :])
                    link(last)

                top16(G, top_s, top_i, s, rest)
                grid = [P, PEER_H, PEER_K, PEER_K]
                ts = top_s[:, :, :].rearrange("p (h c) k -> p h c k", c=2)
                ti = top_i[:, :, :].rearrange("p (h c) k -> p h c k", c=2)
                cand = MTf[:, 2048:4096]
                link(V.tensor_tensor(cand.rearrange("p (h a b) -> p h a b", a=PEER_K, b=PEER_K),
                                     ts[:, :, 0, :].unsqueeze(3).broadcast_to(grid),
                                     ts[:, :, 1, :].unsqueeze(2).broadcast_to(grid), ALU.add))
                spare = PR[:, 6144:8192]
                top16(PEER_H, best_s, best_j, cand.rearrange("p (h n) -> p h n", h=PEER_H),
                      spare.rearrange("p (h n) -> p h n", h=PEER_H))
                gt = gate[:, b, :].rearrange("p (h k) -> p h k", k=PEER_K)
                if layer * NB + b >= 1 and b == 0:
                    dve.wait_ge(ring_free, RING + 4 * SLOTS * layer)
                V.tensor_tensor(gt, best_s[:, :, :], best_s[:, :, 0:1].broadcast_to([P, PEER_H, PEER_K]),
                                ALU.subtract).then_inc(best_ready, 1)
                bj = best_j[:, :, :].rearrange("p h k -> p (h k)")
                V.tensor_single_scalar(half_j[:, 0, :], bj, 4, ALU.logical_shift_right)
                link(V.tensor_single_scalar(half_j[:, 1, :], bj, 15, ALU.bitwise_and))
                for c in range(2):
                    hot = MTf[:, 0:2048]
                    link(V.tensor_tensor(hot.rearrange("p (s a) -> p s a", a=PEER_K),
                                         half_j[:, c, :].unsqueeze(2).broadcast_to([P, SLOTS, PEER_K]),
                                         iota16[:, :].unsqueeze(1).broadcast_to([P, SLOTS, PEER_K]), ALU.is_equal))
                    link(V.tensor_tensor(spare.rearrange("p (h k a) -> p h k a", k=PEER_K, a=PEER_K),
                                         hot.rearrange("p (h k a) -> p h k a", k=PEER_K, a=PEER_K),
                                         ti[:, :, c, :].unsqueeze(2).broadcast_to(grid), ALU.mult))
                    link(V.reduce_sum(half_i[:, c, :], spare.rearrange("p (s a) -> p s a", a=PEER_K), AX.X))
                link(V.scalar_tensor_tensor(out=eidx[:, b, :], in0=half_i[:, 0, :], scalar=float(NKEY),
                                            in1=half_i[:, 1, :], op0=ALU.mult, op1=ALU.add))
                dve.wait_ge(gexp_done, layer * NB + b + 1)
                link(V.reduce_sum(gsum[:, 0, :], gt, AX.X))
                link(V.reciprocal(gsum[:, 1, :], gsum[:, 0, :]))
                V.tensor_tensor(gt, gt, gsum[:, 1, :].unsqueeze(2).broadcast_to([P, PEER_H, PEER_K]),
                                ALU.mult).then_inc(routed, 1)
                dve.wait_ge(routed, layer * NB + b + 1)

            def expert_dots(layer, b, phase):
                o = layer * NB + b
                with dve.Fori(0, PEER_H) as i:
                    for s in range(PEER_K):
                        if s == 0:
                            dve.wait_ge(dots_saved, i + (PEER_H * o + 1))
                            dve.nop(nofuse=True)
                        dve.wait_ge(ring_free, i * PEER_K + (phase * SLOTS + s + RING - 1))
                        dve.wait_ge(landed[s % RING], i * 32 + 16 * (phase * SLOTS // RING + s // RING + 1))
                        V.tensor_tensor_reduce(out=MTf[:, (s % 2) * D:(s % 2 + 1) * D], in0=ring[:, s % RING, :],
                                               in1=H[:, b, :], scale=1.0, scalar=0.0, op0=ALU.mult, op1=ALU.add,
                                               accum_out=dots16[:, s:s + 1]).then_inc(ring_free, 1)
                    dve.wait_ge(ring_free, i * PEER_K + (phase * SLOTS + PEER_K + RING))
                    V.tensor_copy(dots[:, bass.ds(i * PEER_K, PEER_K)], dots16[:, :]).then_inc(dots_saved, 1)
                dve.wait_ge(dots_saved, PEER_H * (o + 1) + 1)
                V.tensor_copy(wgt[:, 0:1], dots[:, 0:1]).then_inc(dots_ready, 1)
                dve.wait_ge(gelu_ready, o + 1)
                link(V.tensor_tensor(wgt[:, :], gelu[:, :], gate[:, b, :], ALU.mult))

            def expert_sum(layer, b, phase):
                with dve.Fori(0, PEER_H) as i:
                    for s in range(PEER_K):
                        dve.wait_ge(ring_free, i * PEER_K + (phase * SLOTS + s + RING))
                        dve.wait_ge(landed[s % RING], i * 32 + 16 * (phase * SLOTS // RING + s // RING + 1))
                        V.scalar_tensor_tensor(out=X[:, b, :], in0=ring[:, s % RING, :],
                                               scalar=wgt[:, bass.ds(i * PEER_K + s, 1)], in1=X[:, b, :],
                                               op0=ALU.mult, op1=ALU.add).then_inc(ring_free, 1)
                dve.wait_ge(ring_free, (phase + 1) * SLOTS + RING)

            def experts(layer):
                norm(2 * layer + 1)
                for b in range(NB):
                    route(layer, b)
                for b in range(NB):
                    expert_dots(layer, b, layer * 4 + b * 2)
                    expert_sum(layer, b, layer * 4 + b * 2 + 1)
                norm(2 * layer + 2)

            V.memset(dots16[:, :], 0.0).then_inc(dots_saved, 1)
            norm(0)
            dve.wait_ge(chunk_copied, 3)
            link(rope(QKV[:, :, 0:1280], 20, 64))
            kd = kdup[:, :].rearrange("p (b g n) -> p b g n", b=NB, g=4)
            for b in range(NB):
                for c in range(2):
                    last = V.tensor_copy(kd[:, b, :, c * 64:(c + 1) * 64],
                                         QKV[:, b, 1024:1280].rearrange("p (g d) -> p g d", g=4))
            last.then_inc(roped, 1)
            dve.wait_ge(consts_ready, 1)
            attention(0)
            add_chunks("out0", 0)
            experts(0)
            inverse_root(Q_RANK, cq_sq, 2, cq_var, cq_root, 1)
            for b in range(NB):
                last = V.scalar_tensor_tensor(out=C1[:, b, 0:CH], in0=C1[:, b, 0:CH], scalar=stat[:, 5, b:b + 1],
                                              in1=gain_q[:, :], op0=ALU.mult, op1=ALU.mult)
            last.then_inc(cq_ready, 1)
            dve.wait_ge(cq_ready, 1)
            dve.wait_ge(chunk_copied, 21)
            link(rope(UQ[:, :, 0:2048], HEADS, P))
            link(rope(UQ[:, :, 2048:3072], HEADS, 64))
            link(rope(C1[:, :, 512:640], 1, P))
            link(rope(C1[:, :, 768:832], 1, 64))
            for c in range(2):
                V.tensor_copy(kdup[:, 0:T].rearrange("p (b n) -> p b n", b=NB)[:, :, c * 64:(c + 1) * 64],
                              C1[:, :, 768:832])
            for b in range(NB):
                last = V.tensor_scalar(iw[:, b, :].rearrange("p (g o e) -> p g o e", o=2, e=2),
                                       C1[:, b, 832:848].rearrange("p (g e o) -> p g o e", o=2, e=2),
                                       float(HEADS) ** -0.5 * 64.0 ** -0.5, None, ALU.mult)
            last.then_inc(roped, 1)
            dve.wait_ge(roped, 2)
            for b in range(NB):
                n = (b + 1) * P
                for g in range(4):
                    j = 4 * b + g
                    dve.wait_ge(ix_done, j + 1)
                    src = ps[:, (j % 2) * 1024:(j % 2 + 1) * 1024].rearrange("p (h k) -> p h k", h=4)[:, :, 0:n]
                    V.scalar_tensor_tensor(out=IXL[:, 4 * g:4 * g + 4, 0:n], in0=src, scalar=0.0,
                                           in1=iw[:, b, 4 * g:4 * g + 4].unsqueeze(2).broadcast_to([P, 4, n]),
                                           op0=ALU.max, op1=ALU.mult).then_inc(ix_read, 1)
                dve.wait_ge(ix_read, 4 * b + 4)
                link(V.reduce_sum(score[:, 0:n], IXL[:, :, 0:n].rearrange("p h k -> p k h"), AX.X))
                link(V.tensor_tensor(score[:, n - P:n], score[:, n - P:n], band[:, P:T], ALU.add))
                for _ in range(TOPK_KEYS // 8):
                    link(V.max(max8[:, :], score[:, 0:n]))
                    link(V.match_replace(score[:, 0:n], max8[:, :], score[:, 0:n], TAKEN))
                link(V.tensor_scalar(keep[:, b, 0:n], score[:, 0:n], TAKEN / 2, NEG, ALU.is_gt, ALU.mult))
                link(V.tensor_tensor(keep[:, b, n - P:n], keep[:, b, n - P:n], band[:, P:T], ALU.add))
            attention(1)
            add_chunks("out1", 1)
            experts(1)


NAMES = ["x", "positions", "norm_mix0", "w_in0", "sinks0", "conv_w0", "w_out0", "norm_ffn0", "peer_wq0",
         "peer_keys0", "peer_u0", "peer_v0", "norm_mix1", "w_in1", "g_qa1", "w_uq1", "w_out1", "norm_ffn1",
         "peer_wq1", "peer_keys1", "peer_u1", "peer_v1", "norm_final"]


def kernel(**inputs):
    import concourse.bacc as _bacc
    from concourse.bass_utils import run_bass_kernel_spmd as _run

    nc = _bacc.Bacc("TRN2", target_bir_lowering=False, num_devices=1)
    arrays, args = {}, []
    for name in NAMES:
        a = np.ascontiguousarray(inputs[name])
        arrays[f"in_{name}"] = a
        args.append(nc.dram_tensor(f"in_{name}", a.shape, mybir.dt.from_np(a.dtype), kind="ExternalInput").ap())
    args.append(nc.dram_tensor("out", (1, T, D), mybir.dt.float32, kind="ExternalOutput").ap())
    program(nc, *args)
    r = _run(nc, [arrays], core_ids=[0])
    return r.results[0]["out"]
```

```python
from contextlib import ExitStack

import numpy as np

import concourse.bass as bass
from concourse import mybir

P = 128
D = 2048
T = 256
NB = T // P
KT_ = D // P
CH = 512
EPS = 1e-5
NEG = -1e30
TAKEN = -3e38
ROPE_THETA = 500000.0
HALF_ROT = 16
CONV_COLS = 1024
Q_RANK = 512
IN1_COLS = 848
TOPK_KEYS = 64
HEADS = 16
PEER_H = 8
PEER_K = 16
NKEY = 128
SLOTS = PEER_H * PEER_K
RING = 8
WSLOTS = 4

TR_LAYER0 = [("h0", 8), ("qk0", 6), ("keys0", 4), ("h1", 8)]
TR_LAYER1 = [("h2", 4), ("cq", 1), ("qk1", 7), ("keys1", 4), ("h3", 4)]
PROJ0 = [("in0_qkv", 6, 3), ("in0_conv", 12, 0), ("out0", 8, 4), ("wq0", 8, 4)]
PROJ1 = [("in1", 8, 2), ("uq", 6, 6), ("out1", 16, 4), ("wq1", 16, 4)]
CONV_ORDER = (2, 3, 4, 5, 0, 1)
HALVES = 2 * len(CONV_ORDER)
CONV_BESIDE = [(2, 3), (4, 5), (6,), (7,), (8,), (9,), (10,), (11,)]
NORMS = [(0, (0, 1)), (1, (0, 1)), (2, (0,)), (3, (0,)), (2, (1,)), (3, (1,)), (4, (0, 1))]

HEAD_OF_PLACE = [(0, 2, 1, 3), (0, 1, 2, 3)]


def before(table, name, col=1):
    n = 0
    for row in table:
        if row[0] == name:
            return n
        n += row[col]
    return n


def total(table, col=1):
    return sum(row[col] for row in table)


def tr_before(stage, b=0):
    if stage in dict(TR_LAYER0):
        return before(TR_LAYER0, stage)
    return total(TR_LAYER0) + b * total(TR_LAYER1) + before(TR_LAYER1, stage)


def chunk_before(name, b=0):
    if name in [p[0] for p in PROJ0]:
        return before(PROJ0, name, 2)
    return total(PROJ0, 2) + b * total(PROJ1, 2) + before(PROJ1, name, 2)


def copied_before(name, b=0):
    def copied(table, upto):
        return sum(p[2] for p in table[:upto] if not p[0].startswith("out"))
    names = [p[0] for p in PROJ0]
    if name in names:
        return copied(PROJ0, names.index(name))
    return copied(PROJ0, 4) + b * copied(PROJ1, 4) + copied(PROJ1, [p[0] for p in PROJ1].index(name))


def norm_before(n):
    return sum(len(blocks) for _, blocks in NORMS[:n])


def program(nc, x, positions, norm_mix0, w_in0, sinks0, conv_w0, w_out0, norm_ffn0, peer_wq0,
            peer_keys0, peer_u0, peer_v0, norm_mix1, w_in1, g_qa1, w_uq1, w_out1, norm_ffn1,
            peer_wq1, peer_keys1, peer_u1, peer_v1, norm_final, out):
    fp32 = mybir.dt.float32
    bf16 = mybir.dt.bfloat16
    u32 = mybir.dt.uint32
    i32 = mybir.dt.int32
    ALU = mybir.AluOpType
    ACT = mybir.ActivationFunctionType
    AX = mybir.AxisListType
    ctx = ExitStack()
    with ctx:
        def sb(name, shape, dt=fp32):
            return ctx.enter_context(nc.sbuf_tensor(name, shape, dt))

        def sem(name):
            return ctx.enter_context(nc.semaphore(name))

        X = sb("X", [P, NB, D])
        H = sb("H", [P, NB, D])
        HT = sb("HT", [P, KT_, T])
        MT = sb("MT", [P, KT_, T])
        PR = sb("PR", [P, 9216])
        A = sb("A", [P, 4096])
        ring = sb("ring", [P, RING, D])
        gain = sb("gain", [P, D])
        gain_q = sb("gain_q", [P, Q_RANK])
        kdup = sb("kdup", [P, 1024])
        KT = sb("KT", [P, 1024])
        ident = sb("ident", [P, P])
        band = sb("band", [P, T])
        keep = sb("keep", [P, T])
        VB = sb("VB", [P, NB, P])
        ikdup = sb("ikdup", [P, P])
        iota16 = sb("iota16", [P, PEER_K])
        sinks_in = sb("sinks_in", [P, HEADS])
        sinks = sb("sinks", [P, HEADS])
        conv_w = sb("conv_w", [P, 3, 8])
        pos_i = sb("pos_i", [P, NB], i32)
        pos_f = sb("pos_f", [P, NB])
        cosT = sb("cosT", [P, NB, HALF_ROT])
        sinT = sb("sinT", [P, NB, HALF_ROT])
        ang = sb("ang", [P, NB, HALF_ROT])
        turns = sb("turns", [P, NB, HALF_ROT])
        stat = sb("stat", [P, 8, NB])
        soft = sb("soft", [P, 2, 6, 4])
        iw = sb("iw", [P, NB, HEADS])
        score = sb("score", [P, T])
        max8 = sb("max8", [P, 8])
        gsum = sb("gsum", [P, 2, PEER_H])
        gate = sb("gate", [P, NB, SLOTS])
        eidx = sb("eidx", [P, NB, SLOTS], u32)
        cur = sb("cur", [P, 2, 8], u32)
        dots16 = sb("dots16", [P, PEER_K])
        dots = sb("dots", [P, SLOTS])
        wgt = sb("wgt", [P, SLOTS])
        ps = ctx.enter_context(nc.psum_tensor("ps", [P, 8 * 512], fp32))

        def flat(t):
            return t[:, :, :].rearrange("p a b -> p (a b)")

        Hf, MTf = flat(H), flat(MT)
        QKV = PR[:, 0:3072].rearrange("p (b n) -> p b n", b=NB)
        GATES = PR[:, 3072:9216].rearrange("p (g t) -> p g t", t=T)
        PQT0 = PR[:, 0:4096].rearrange("p (g t) -> p g t", t=T)
        PKT0 = PR[:, 4096:6144].rearrange("p (g n) -> p g n", n=NKEY)
        PKN0 = PR[:, 6144:8192].rearrange("p (g n) -> p g n", n=NKEY)
        C1, UQ = PR[:, 0:IN1_COLS], PR[:, IN1_COLS:IN1_COLS + 3072]
        PQT1 = PR[:, 0:2048].rearrange("p (g t) -> p g t", t=P)
        PKT1 = PR[:, 2048:4096].rearrange("p (g n) -> p g n", n=NKEY)
        IQT = PR[:, 8192:9216].rearrange("p (g t) -> p g t", t=P)
        HTf = flat(HT)
        HT1 = HTf[:, 0:2048].rearrange("p (k t) -> p k t", t=P)
        QT1 = HTf[:, 2048:4096].rearrange("p (h t) -> p h t", t=P)
        PKN1 = QT1
        MT1 = MTf[:, 0:2048].rearrange("p (k t) -> p k t", t=P)
        QT0 = Hf[:, 2048:4096].rearrange("p (k t) -> p k t", t=T)
        rope_tmp0 = Hf[:, 0:2048].rearrange("p (k n) -> p k n", k=4)
        rope_tmp1 = MTf[:, 1024:2048].rearrange("p (k n) -> p k n", k=4)
        SC = [[A[:, 0:1024], A[:, 1024:2048]], [A[:, 0:1024]] * 2]
        PT = [[A[:, 2048:3072], A[:, 3072:4096]], [A[:, 1024:2048]] * 2]
        SC, PT = ([[t.rearrange("p (h k) -> p h k", h=4) for t in pair] for pair in both] for both in (SC, PT))
        IXL = A[:, 0:1024].rearrange("p (h k) -> p h k", h=4)
        ixsum = A[:, 1024:1024 + T]
        junk = kdup[:, :].bitcast(bf16)
        def inA(at, groups, n):
            return A[:, at:at + groups * n].rearrange("p (g n) -> p g n", n=n)

        top_s, top_i = inA(0, 2 * PEER_H, PEER_K), inA(256, 2 * PEER_H, PEER_K).bitcast(u32)
        best_s, best_j = inA(512, PEER_H, PEER_K), inA(640, PEER_H, PEER_K).bitcast(u32)
        gelu = A[:, 1280:1280 + SLOTS]
        half_j, half_i = inA(768, 2, SLOTS).bitcast(u32), inA(1024, 2, SLOTS)
        wring = ring[:, :, :].rearrange("p (s two) n -> p s (two n)", two=2)

        def wtile(slot):
            return wring[:, slot, :].rearrange("p (k n) -> p k n", n=CH)

        ltiles = [t.rearrange("p (k n) -> p k n", n=CH) for t in
                  (PR[:, 4096:6144], PR[:, 6144:8192], A[:, 2048:4096], MTf[:, 2048:4096])]

        def bank(i, n=1, w=512):
            return ps[:, i * 512:(i + n - 1) * 512 + w]

        x_loaded, gain_loaded, small_loaded = sem("x_loaded"), sem("gain_loaded"), sem("small_loaded")
        keys_loaded, out_stored = sem("keys_loaded"), sem("out_stored")
        w_loaded = [sem(f"w_loaded{i}") for i in range(WSLOTS)]
        w_used = sem("w_used")
        l_loaded = [sem(f"l_loaded{i}") for i in range(WSLOTS)]
        l_used = sem("l_used")
        keys1_loaded = sem("keys1_loaded")
        consts_ready = sem("consts_ready")
        conv_done = sem("conv_done")
        angles_ready, sines_ready = sem("angles_ready"), sem("sines_ready")
        sq_done, var_ready, root_ready, h_ready = (sem("sq_done"), sem("var_ready"),
                                                   sem("root_ready"), sem("h_ready"))
        cq_sq, cq_var, cq_root, cq_ready = sem("cq_sq"), sem("cq_var"), sem("cq_root"), sem("cq_ready")
        tr_done, tr_copied = sem("tr_done"), sem("tr_copied")
        chunk_done, chunk_copied, chunk_added = sem("chunk_done"), sem("chunk_copied"), sem("chunk_added")
        half_done, half_copied = sem("half_done"), sem("half_copied")
        roped = sem("roped")
        ix_done, ix_read = sem("ix_done"), sem("ix_read")
        sc_done, sc_read, exp_done, prob_ready = (sem("sc_done"), sem("sc_read"), sem("exp_done"),
                                                  sem("prob_ready"))
        pt_done, pt_copied, pv_done, pv_copied = (sem("pt_done"), sem("pt_copied"), sem("pv_done"),
                                                  sem("pv_copied"))
        rs_done, best_ready, gexp_done, routed = (sem("rs_done"), sem("best_ready"),
                                                  sem("gexp_done"), sem("routed"))
        idx_cur = sem("idx_cur")
        landed = [sem(f"landed{i}") for i in range(RING)]
        ring_free = sem("ring_free")
        dots_saved, dots_ready, gelu_ready = sem("dots_saved"), sem("dots_ready"), sem("gelu_ready")
        vec_step, act_step, pool_step = sem("vec_step"), sem("act_step"), sem("pool_step")

        gains = [norm_mix0, norm_ffn0, norm_mix1, norm_ffn1, norm_final]
        keys_dram = [peer_keys0, peer_keys1]
        u_dram, v_dram = [peer_u0, peer_u1], [peer_v0, peer_v1]

        def transposes(stage, b=0):
            def pack(srcs, dst):
                return [(srcs[i:i + 4], dst(i)) for i in range(0, len(srcs), 4)]

            def cols(t, n, at=0):
                return [t[:, at + k * P:at + (k + 1) * P] for k in range(n)]

            if stage in ("h0", "h1"):
                return [e for c in range(NB) for e in pack(
                    cols(H[:, c, :], KT_), lambda i, c=c: HT[:, i:i + 4, c * P:(c + 1) * P])]
            if stage in ("h2", "h3"):
                return pack(cols(H[:, b, :], KT_), lambda i: HT1[:, i:i + 4, :])
            if stage == "keys0":
                return pack([PKN0[:, g, :] for g in range(2 * PEER_H)], lambda i: PKT0[:, i:i + 4, :])
            if stage == "keys1":
                return pack([PKN1[:, g, :] for g in range(2 * PEER_H)], lambda i: PKT1[:, i:i + 4, :])
            if stage == "cq":
                return pack(cols(C1, Q_RANK // P), lambda i: MT1[:, i:i + 4, :])
            if stage == "qk0":
                kd = kdup[:, :].rearrange("p (b g n) -> p b g n", b=NB, g=4)
                kt = KT[:, :].rearrange("p (g t) -> p g t", g=4)
                return [e for c in range(NB) for e in
                        pack(cols(QKV[:, c, :], 8), lambda i, c=c: QT0[:, i:i + 4, c * P:(c + 1) * P])
                        + pack([kd[:, c, g, :] for g in range(4)],
                               lambda i, c=c: kt[:, :, c * P:(c + 1) * P])]
            kt = KT[:, 0:2 * T].rearrange("p (g t) -> p g t", g=2)
            return (pack(cols(UQ, HEADS), lambda i: QT1[:, i:i + 4, :])
                    + pack(cols(UQ, 8, 2048), lambda i: IQT[:, i:i + 4, :])
                    + pack([C1[:, 512:640], ikdup[:, :]], lambda i: kt[:, :, b * P:(b + 1) * P]))

        block = ctx.enter_context(nc.Block())

        @block.sync
        def _(sp):
            for b in range(NB):
                sp.dma_start(X[:, b, :], x[0, b * P:(b + 1) * P, :]).then_inc(x_loaded, 16)
            sp.dma_start(gain[:, :], gains[0].partition_broadcast(P)).then_inc(small_loaded, 16)
            with nc.allow_non_contiguous_dma(reason="a few small vectors laid over the partitions"):
                sp.dma_start(pos_i[:, :], positions.rearrange("o (b p) -> p (o b)", p=P)).then_inc(small_loaded, 16)
            sp.dma_start(sinks_in[:, :], sinks0.partition_broadcast(P)).then_inc(small_loaded, 16)
            with nc.allow_non_contiguous_dma(reason="a few small vectors laid over the partitions"):
                sp.dma_start(conv_w[:, :, :], conv_w0.rearrange("w (c p) -> p w c", p=P)).then_inc(small_loaded, 16)
            sp.dma_start(gain_q[:, :], g_qa1.partition_broadcast(P)).then_inc(small_loaded, 16)

            def load_chunks(n0, w, c0, chunks):
                w = w.rearrange("(h k p) n -> h p k n", h=2, p=P)
                with sp.Fori(0, chunks // 2) as i:
                    for c in range(2):
                        for h in range(2):
                            n = n0 + 2 * c + h
                            sp.wait_ge(w_used, i * 4 + (n - WSLOTS + 1))
                            sp.dma_start(wtile(n % WSLOTS), w[h][:, :, bass.ds((i * 2 + (c0 + c)) * CH, CH)]
                                         ).then_inc(w_loaded[n % WSLOTS], 16)

            def load_gain(n):
                sp.wait_ge(h_ready, norm_before(n))
                sp.dma_start(gain[:, :], gains[NORMS[n][0]].partition_broadcast(P)).then_inc(gain_loaded, 16)

            w = w_in0.rearrange("(h k p) n -> h p k n", h=2, p=P)
            for n in range(6):
                if n >= WSLOTS:
                    sp.wait_ge(w_used, n - WSLOTS + 1)
                sp.dma_start(wtile(n % WSLOTS), w[n % 2][:, :, (n // 2) * CH:(n // 2 + 1) * CH]
                             ).then_inc(w_loaded[n % WSLOTS], 16)
            load_gain(1)
            n0 = before(PROJ0, "in0_conv")
            load_chunks(n0, w_in0, 3 + CONV_ORDER[0], 4)
            load_chunks(n0 + 8, w_in0, 3 + CONV_ORDER[4], 2)
            load_chunks(before(PROJ0, "out0"), w_out0, 0, 4)
            load_chunks(before(PROJ0, "wq0"), peer_wq0, 0, 4)

            def load_quarters(name, b, w):
                w = w.rearrange("(q k p) n -> q p k n", q=4, p=P)
                n0 = b * total(PROJ1) + before(PROJ1, name)
                with sp.Fori(0, 4) as i:
                    for q in range(4):
                        s = (n0 + q) % WSLOTS
                        sp.wait_ge(l_used, i * 4 + (n0 + q - WSLOTS + 1))
                        sp.dma_start(ltiles[s], w[q][:, :, bass.ds(i * CH, CH)]).then_inc(l_loaded[s], 16)

            for b in range(NB):
                sp.wait_ge(routed, b + 2)
                load_gain(2 + 2 * b)
                n = b * total(PROJ1)
                w = w_in1.rearrange("(q k p) n -> q p k n", q=4, p=P)
                for c, width in enumerate((CH, IN1_COLS - CH)):
                    for q in range(4):
                        if n >= WSLOTS:
                            sp.wait_ge(l_used, n - WSLOTS + 1)
                        sp.dma_start(ltiles[n % WSLOTS][:, :, 0:width], w[q][:, :, c * CH:c * CH + width]
                                     ).then_inc(l_loaded[n % WSLOTS], 16)
                        n += 1
                load_gain(3 + 2 * b)
                w = w_uq1.rearrange("(k p) n -> p k n", p=P)
                for c in range(6):
                    sp.wait_ge(l_used, n - WSLOTS + 1)
                    sp.dma_start(ltiles[n % WSLOTS], w[:, :, c * CH:(c + 1) * CH]).then_inc(l_loaded[n % WSLOTS], 16)
                    n += 1
                load_quarters("out1", b, w_out1)
                sp.wait_ge(pv_done, 8 + 4 * (b + 1))
                sp.dma_start(PKN1, peer_keys1.rearrange("h c n d -> n (h c) d")).then_inc(keys1_loaded, 16)
                load_quarters("wq1", b, peer_wq1)
            load_gain(6)
            sp.wait_ge(h_ready, norm_before(7))
            for b in range(NB):
                sp.dma_start(out[0, b * P:(b + 1) * P, :], H[:, b, :]).then_inc(out_stored, 16)
            sp.wait_ge(out_stored, 16 * NB)

        @block.gpsimd
        def _(pool):
            steps = [0]

            def link(ins):
                steps[0] += 1
                ins.then_inc(pool_step, 1)
                pool.wait_ge(pool_step, steps[0])

            nc.gpsimd.iota(iota16[:, :], pattern=[[1, PEER_K]], base=0, channel_multiplier=0,
                           allow_small_or_imprecise_dtypes=True)
            nc.gpsimd.memset(ident[:, :], 0.0)
            link(nc.gpsimd.memset(band[:, :], 0.0))
            nc.gpsimd.affine_select(out=ident[:, :], in_=ident[:, :], compare_op=ALU.not_equal, fill=1.0,
                                    base=0, pattern=[[-1, P]], channel_multiplier=1)
            nc.gpsimd.affine_select(out=band[:, 0:P], in_=band[:, 0:P], compare_op=ALU.is_gt, fill=NEG,
                                    base=0, pattern=[[1, P]], channel_multiplier=-1)
            nc.gpsimd.affine_select(out=band[:, P:T], in_=band[:, P:T], compare_op=ALU.is_ge, fill=NEG,
                                    base=0, pattern=[[-1, P]], channel_multiplier=1).then_inc(consts_ready, 1)

            bg, cg, hx = (GATES[:, 8 * i:8 * i + 8, :] for i in range(3))
            tmp = MT[:, 8:16, :]

            def tap(w):
                return conv_w[:, w, :].unsqueeze(2).broadcast_to([P, 8, T])

            pool.wait_ge(small_loaded, 80)
            pool.wait_ge(half_copied, 8)
            link(nc.gpsimd.tensor_tensor(cg, cg, hx, ALU.mult))
            nc.gpsimd.tensor_tensor(hx, cg, tap(2), ALU.mult)
            link(nc.gpsimd.tensor_tensor(tmp, cg, tap(1), ALU.mult))
            link(nc.gpsimd.tensor_tensor(hx[:, :, 1:T], hx[:, :, 1:T], tmp[:, :, 0:T - 1], ALU.add))
            link(nc.gpsimd.tensor_tensor(tmp, cg, tap(0), ALU.mult))
            link(nc.gpsimd.tensor_tensor(hx[:, :, 2:T], hx[:, :, 2:T], tmp[:, :, 0:T - 2], ALU.add))
            pool.wait_ge(half_copied, HALVES)
            nc.gpsimd.tensor_tensor(tmp, hx, bg, ALU.mult).then_inc(conv_done, 1)

            pool.wait_ge(pv_done, 8)
            pool.wait_ge(conv_done, 1)
            pool.dma_start(PKN0, peer_keys0.rearrange("h c n d -> n (h c) d")).then_inc(keys_loaded, 16)

            def gather(layer, b, table, phase):
                with pool.Fori(0, PEER_H) as i:
                    for o in range(2):
                        nc.gpsimd.tensor_copy(cur[:, o, :], eidx[:, b, bass.ds(i * 16 + o * 8, 8)]).then_inc(idx_cur, 1)
                        pool.wait_ge(idx_cur, i * 2 + (phase * 16 + o + 1))
                        pool.nop(nofuse=True)
                        for r in range(RING):
                            pool.wait_ge(ring_free, i * 16 + (phase * SLOTS + o * 8 + r + 1))
                            pool.nop(nofuse=True)
                            pool.indirect_dma_start(ring[:, r, :], None, table,
                                                    bass.IndirectOffsetOnAxis(cur[:, o, r:r + 1], 0)).then_inc(landed[r], 16)

            pool.wait_ge(w_used, total(PROJ0))
            for layer in range(2):
                for b in range(NB):
                    pool.wait_ge(routed, layer * NB + b + 1)
                    gather(layer, b, u_dram[layer], layer * 4 + b * 2)
                    gather(layer, b, v_dram[layer], layer * 4 + b * 2 + 1)

        @block.scalar
        def _(act):
            steps = [0]

            def link(ins):
                steps[0] += 1
                ins.then_inc(act_step, 1)
                act.wait_ge(act_step, steps[0])

            act.wait_ge(angles_ready, 1)
            nc.scalar.activation(sinT[:, :, :], ang[:, :, :], ACT.Sin)
            nc.scalar.activation(cosT[:, :, :], ang[:, :, :], ACT.Sin, scale=0.5).then_inc(sines_ready, 1)

            def squares(n):
                for b in NORMS[n][1]:
                    nc.scalar.activation(H[:, b, :], X[:, b, :], ACT.Square,
                                         accum_out=stat[:, 0, b:b + 1]).then_inc(sq_done, 1)
                act.wait_ge(var_ready, n + 1)
                bs = slice(NORMS[n][1][0], NORMS[n][1][-1] + 1)
                nc.scalar.activation(stat[:, 3, bs], stat[:, 2, bs], ACT.Sqrt).then_inc(root_ready, 1)

            def copy_transposes(stage, b=0):
                n0 = tr_before(stage, b)
                for n, (srcs, dst) in enumerate(transposes(stage, b)):
                    act.wait_ge(tr_done, n0 + n + 1)
                    nc.scalar.copy(dst, bank(n, w=len(srcs) * P).rearrange("p (g n) -> p g n", n=P)).then_inc(tr_copied, 1)

            def copy_channels(name, dst, chunks, tokens=T, b=0):
                m0 = chunk_before(name, b)
                with act.Fori(0, chunks // 2) as i:
                    for c in range(2):
                        act.wait_ge(chunk_done, i * 2 + (m0 + c + 1))
                        src = bank(4 * ((m0 + c) % 2), 4).rearrange("p (g n) -> p g n", n=512)[:, :, 0:tokens]
                        nc.scalar.copy(dst[:, bass.ds(i * 8 + c * 4, 4), :], src).then_inc(chunk_copied, 1)

            def exps(layer, q):
                act.wait_ge(sc_read, q + 1)
                pr, nk = q % 2, (q % 8) // 4 + 1
                s = SC[layer][pr]
                for h in range(4):
                    last = nc.scalar.activation(s[:, h, 0:nk * P], s[:, h, 0:nk * P], ACT.Exp,
                                                bias=soft[:, pr, 0, h:h + 1], accum_out=soft[:, pr, 1, h:h + 1])
                if layer == 0:
                    last = nc.scalar.activation(soft[:, pr, 3, :], soft[:, pr, 2, :], ACT.Exp)
                last.then_inc(exp_done, 1)

            def copy_out(layer, q):
                pr, b, g, nk = q % 2, (q % 8) // 4, q % 4, (q % 8) // 4 + 1
                act.wait_ge(pt_done, q + 1)
                if layer == 1 or q >= 2:
                    act.wait_ge(pv_done, q - 1 + layer)
                src = bank(2, 2).rearrange("p (h n) -> p h n", h=4)[:, :, 0:nk * P]
                nc.scalar.copy(PT[layer][pr][:, :, 0:nk * P], src).then_inc(pt_copied, 1)
                act.wait_ge(pv_done, q + 1)
                n = (2, 4)[layer]
                dst = MT1[:, 4 * g:4 * g + 4, :] if layer else MT[:, 2 * g:2 * g + 2, b * P:(b + 1) * P]
                nc.scalar.copy(dst, bank(4 + pr, w=n * P).rearrange("p (h n) -> p h n", h=n)).then_inc(pv_copied, 1)

            def gate_exp(layer, b):
                act.wait_ge(best_ready, layer * NB + b + 1)
                nc.scalar.activation(gate[:, b, :], gate[:, b, :], ACT.Exp).then_inc(gexp_done, 1)

            def gelus(layer, b):
                act.wait_ge(dots_ready, layer * NB + b + 1)
                nc.scalar.activation(gelu[:, :], dots[:, :], ACT.Gelu).then_inc(gelu_ready, 1)

            act.wait_ge(x_loaded, 32)
            squares(0)
            copy_transposes("h0")
            for c in range(3):
                act.wait_ge(chunk_done, c + 1)
                for b in range(NB):
                    last = nc.scalar.copy(QKV[:, b, c * CH:(c + 1) * CH], bank(4 * (c % 2) + b))
                last.then_inc(chunk_copied, 1)

            def copy_half(n):
                act.wait_ge(half_done, n + 1)
                g = 4 * CONV_ORDER[n // 2] + 2 * (n % 2)
                nc.scalar.copy(GATES[:, g:g + 2, :], bank(6 + n % 2).rearrange("p (g t) -> p g t", t=T)
                               ).then_inc(half_copied, 1)

            copy_half(0)
            copy_half(1)
            copy_transposes("qk0")
            exps(0, 0)
            for q in range(8):
                if q < 7:
                    exps(0, q + 1)
                for n in CONV_BESIDE[q]:
                    copy_half(n)
                copy_out(0, q)
            copy_transposes("keys0")
            act.wait_ge(chunk_added, 2 + 4)
            squares(1)
            copy_transposes("h1")
            copy_channels("wq0", PQT0, 4)
            for b in range(NB):
                gate_exp(0, b)
            gelus(0, 0)

            def copy_token_chunk(m, dst, width=CH):
                act.wait_ge(chunk_done, m + 1)
                nc.scalar.copy(dst, bank(4 * (m % 2), w=width)).then_inc(chunk_copied, 1)

            for b in range(NB):
                act.wait_ge(ring_free, RING + 2 * SLOTS * (b + 1))
                squares(2 + 2 * b)
                copy_transposes("h2", b)
                m0 = chunk_before("in1", b)
                copy_token_chunk(m0, C1[:, 0:CH])
                act.wait_ge(chunk_done, m0 + 2)
                nc.scalar.copy(VB[:, b, :], bank(4 * ((m0 + 1) % 2))[:, P:2 * P])
                copy_token_chunk(m0 + 1, C1[:, CH:IN1_COLS], IN1_COLS - CH)
                act.wait_ge(chunk_copied, copied_before("uq", b))
                nc.scalar.activation(A[:, 0:CH], C1[:, 0:CH], ACT.Square,
                                     accum_out=stat[:, 0, b:b + 1]).then_inc(cq_sq, 1)
                act.wait_ge(cq_var, b + 1)
                nc.scalar.activation(stat[:, 3, b:b + 1], stat[:, 2, b:b + 1], ACT.Sqrt).then_inc(cq_root, 1)
                copy_transposes("cq", b)
                m0 = chunk_before("uq", b)
                for c in range(6):
                    copy_token_chunk(m0 + c, UQ[:, c * CH:(c + 1) * CH])
                copy_transposes("qk1", b)
                for q in range(8 + 4 * b, 12 + 4 * b):
                    exps(1, q)
                    copy_out(1, q)
                gelus(b, 1 - b)
                copy_transposes("keys1", b)
                act.wait_ge(chunk_added, 2 + 4 * (b + 2))
                squares(3 + 2 * b)
                copy_transposes("h3", b)
                copy_channels("wq1", PQT1, 4, P, b)
                gate_exp(1, b)
            gelus(1, 1)
            act.wait_ge(ring_free, RING + 8 * SLOTS)
            squares(6)

        @block.tensor
        def _(pe):
            def transpose_stage(stage, b=0):
                n0 = tr_before(stage, b)
                banks = transposes(stage, b)
                for n, (srcs, dst) in enumerate(banks):
                    for i, s in enumerate(srcs):
                        last = nc.tensor.transpose(ps[:, n * 512 + i * P:n * 512 + (i + 1) * P], s, ident[:, :])
                    last.then_inc(tr_done, 1)
                pe.wait_ge(tr_copied, n0 + len(banks))

            def chunk_ends(used, count):
                pe.wait_ge(used, count)
                pe.nop(nofuse=True).then_inc(chunk_done, 1)

            def chunk_tile(m, tile, lhs, k0, count, width=CH, tokens=None):
                for k in range(tile.shape[1]):
                    kk = k0 + k
                    flags = dict(start=(kk == 0), stop=(kk == count - 1))
                    if tokens:
                        for g in range(4):
                            last = nc.tensor.matmul(bank(4 * (m % 2) + g, w=tokens), tile[:, k, g * P:(g + 1) * P],
                                                    lhs[:, kk, :], **flags)
                    else:
                        for b in range(lhs.shape[2] // P):
                            last = nc.tensor.matmul(bank(4 * (m % 2) + b, w=width), lhs[:, kk, b * P:(b + 1) * P],
                                                    tile[:, k, 0:width], **flags)
                return last

            def conv_half(n):
                n0 = before(PROJ0, "in0_conv") + n // 2 * 2
                if n >= 2:
                    pe.wait_ge(half_copied, n - 1)
                for g in (0, 1):
                    at = (6 + n % 2) * 512 + g * T
                    for t in range(2):
                        slot = (n0 + t) % WSLOTS
                        pe.wait_ge(w_loaded[slot], 16 * ((n0 + t) // WSLOTS + 1))
                        for k in range(8):
                            c = (n % 2 * 2 + g) * P
                            last = nc.tensor.matmul(ps[:, at:at + T], wtile(slot)[:, k, c:c + P], HT[:, 8 * t + k, :],
                                                    start=(t == k == 0), stop=(t == 1 and k == 7))
                        if n % 2 and g:
                            last.then_inc(w_used, 1)
                if n % 2:
                    pe.wait_ge(w_used, n0 + 2)
                    pe.nop(nofuse=True).then_inc(half_done, 1)
                else:
                    last.then_inc(half_done, 1)

            def chunk_loop(name, chunks, lhs, tokens, drained, d0):
                n0, m0 = before(PROJ0, name), chunk_before(name)
                with pe.Fori(0, chunks // 2) as i:
                    for c in range(2):
                        pe.wait_ge(drained, i * 2 + (d0 + c - 1))
                        for t in range(2):
                            n = n0 + 2 * c + t
                            pe.wait_ge(w_loaded[n % WSLOTS], i * 16 + 16 * (n // WSLOTS + 1))
                            chunk_tile(m0 + c, wtile(n % WSLOTS), lhs, 8 * t, KT_, tokens=tokens).then_inc(w_used, 1)
                        chunk_ends(w_used, i * 4 + (n0 + 2 * c + 2))

            def quarter_loop(name, b, lhs, tokens, drained, d0):
                n0, m0 = b * total(PROJ1) + before(PROJ1, name), chunk_before(name, b)
                with pe.Fori(0, 2) as i:
                    for c in range(2):
                        pe.wait_ge(drained, i * 2 + (d0 + c - 1))
                        for t in range(4):
                            n = n0 + 4 * c + t
                            pe.wait_ge(l_loaded[n % WSLOTS], i * 32 + 16 * (n // WSLOTS + 1))
                            chunk_tile(m0 + c, ltiles[n % WSLOTS], lhs, 4 * t, KT_, tokens=tokens).then_inc(l_used, 1)
                        chunk_ends(l_used, i * 8 + (n0 + 4 * c + 4))

            def scores(layer, q):
                pr, b, g, nk = q % 2, (q % 8) // 4, q % 4, (q % 8) // 4 + 1
                if q % 8:
                    pe.wait_ge(sc_read, q)
                for i in range(4):
                    h = 4 * g + HEAD_OF_PLACE[layer][i]
                    o = ps[:, i * T:i * T + nk * P]
                    if layer == 0:
                        r = 64 * (h % 2)
                        lhs = QT0[r:r + 64, h // 2, b * P:(b + 1) * P]
                        rhs = KT[r:r + 64, g * T:g * T + nk * P]
                    else:
                        lhs, rhs = QT1[:, h, :], KT[:, 0:nk * P]
                    last = nc.tensor.matmul(o, lhs, rhs, start=True, stop=True)
                last.then_inc(sc_done, 1)

            def values(layer, q):
                pr, b, g, nk = q % 2, (q % 8) // 4, q % 4, (q % 8) // 4 + 1
                pe.wait_ge(prob_ready, q + 1)
                if q >= 1:
                    pe.wait_ge(pt_copied, q)
                for i in range(4):
                    for kb in range(nk):
                        last = nc.tensor.transpose(ps[:, 1024 + i * T + kb * P:1024 + i * T + (kb + 1) * P],
                                                   SC[layer][pr][:, i, kb * P:(kb + 1) * P], ident[:, :])
                last.then_inc(pt_done, 1)
                pe.wait_ge(pt_copied, q + 1)
                if q >= 2:
                    pe.wait_ge(pv_copied, q - 1)
                for i in range(4):
                    h = 4 * g + HEAD_OF_PLACE[layer][i]
                    for kb in range(nk):
                        if layer == 0:
                            r = 64 * (h % 2)
                            c = (4 + pr) * 512 + (h % 4 // 2) * P
                            o = ps[r:r + 64, c:c + P]
                            lhs = QKV[:, kb, 1280 + g * 64:1280 + (g + 1) * 64]
                        else:
                            o = ps[:, (4 + pr) * 512 + i * P:(4 + pr) * 512 + (i + 1) * P]
                            lhs = VB[:, kb, :]
                        last = nc.tensor.matmul(o, lhs, PT[layer][pr][:, i, kb * P:(kb + 1) * P],
                                                start=(kb == 0), stop=(kb == nk - 1))
                last.then_inc(pv_done, 1)

            def attention(layer, q0, n):
                scores(layer, q0)
                for q in range(q0, q0 + n):
                    if q + 1 < q0 + n:
                        scores(layer, q + 1)
                    if layer == 0:
                        for half in CONV_BESIDE[q]:
                            conv_half(half)
                    values(layer, q)
                pe.wait_ge(pv_copied, q0 + n)

            def key_scores(at, queries, keys):
                for g in range(2 * PEER_H):
                    last = nc.tensor.matmul(ps[:, at + g * NKEY:at + (g + 1) * NKEY], queries(g), keys[:, g, :],
                                            start=True, stop=True)
                last.then_inc(rs_done, 1)

            pe.wait_ge(consts_ready, 1)
            pe.wait_ge(h_ready, 2)
            transpose_stage("h0")
            for c in range(3):
                if c >= 2:
                    pe.wait_ge(chunk_copied, c - 1)
                for t in range(2):
                    n = 2 * c + t
                    pe.wait_ge(w_loaded[n % WSLOTS], 16 * (n // WSLOTS + 1))
                    chunk_tile(c, wtile(n % WSLOTS), HT, 8 * t, KT_).then_inc(w_used, 1)
                chunk_ends(w_used, 2 * c + 2)
            pe.wait_ge(chunk_copied, 3)
            conv_half(0)
            conv_half(1)
            pe.wait_ge(roped, 1)
            transpose_stage("qk0")
            attention(0, 0, 8)
            pe.wait_ge(conv_done, 1)
            chunk_loop("out0", 4, MT, None, chunk_added, 2)
            pe.wait_ge(keys_loaded, 16)
            pe.wait_ge(chunk_added, 2 + 4)
            transpose_stage("keys0")
            pe.wait_ge(h_ready, 4)
            transpose_stage("h1")
            chunk_loop("wq0", 4, HT, T, chunk_copied, 3)
            pe.wait_ge(chunk_copied, 7)
            for b in range(NB):
                key_scores(b * 2048, lambda g: PQT0[:, g, b * P:(b + 1) * P], PKT0)
            pe.wait_ge(routed, 2)

            for b in range(NB):
                n, m, done = b * total(PROJ1), chunk_before("in1", b), copied_before("in1", b)
                pe.wait_ge(h_ready, norm_before(3 + 2 * b))
                transpose_stage("h2", b)
                for c, width in enumerate((CH, IN1_COLS - CH)):
                    for t in range(4):
                        pe.wait_ge(l_loaded[n % WSLOTS], 16 * (n // WSLOTS + 1))
                        chunk_tile(m + c, ltiles[n % WSLOTS], HT1, 4 * t, KT_, width).then_inc(l_used, 1)
                        n += 1
                    chunk_ends(l_used, n)
                pe.wait_ge(cq_ready, b + 1)
                pe.wait_ge(chunk_copied, done + 2)
                transpose_stage("cq", b)
                m, done = chunk_before("uq", b), copied_before("uq", b)
                for c in range(6):
                    if c >= 2:
                        pe.wait_ge(chunk_copied, done + c - 1)
                    pe.wait_ge(l_loaded[n % WSLOTS], 16 * (n // WSLOTS + 1))
                    chunk_tile(m + c, ltiles[n % WSLOTS], MT1, 0, 4).then_inc(l_used, 1)
                    n += 1
                    chunk_ends(l_used, n)
                pe.wait_ge(chunk_copied, done + 6)
                pe.wait_ge(roped, 2 + b)
                transpose_stage("qk1", b)
                for g in range(4):
                    if g >= 2:
                        pe.wait_ge(ix_read, 4 * b + g - 1)
                    for i in range(4):
                        h = 4 * g + HEAD_OF_PLACE[0][i]
                        r = 64 * (h % 2)
                        at = (g % 2) * 1024 + i * T
                        last = nc.tensor.matmul(ps[:, at:at + (b + 1) * P], IQT[r:r + 64, h // 2, :],
                                                KT[r:r + 64, T:T + (b + 1) * P], start=True, stop=True)
                    last.then_inc(ix_done, 1)
                pe.wait_ge(ix_read, 4 * b + 4)
                attention(1, 8 + 4 * b, 4)
                quarter_loop("out1", b, MT1, None, chunk_added, 6 + 4 * b)
                pe.wait_ge(keys1_loaded, 16 * (b + 1))
                pe.wait_ge(chunk_added, 2 + 4 * (b + 2))
                transpose_stage("keys1", b)
                pe.wait_ge(h_ready, norm_before(4 + 2 * b))
                transpose_stage("h3", b)
                done = copied_before("wq1", b)
                quarter_loop("wq1", b, HT1, P, chunk_copied, done)
                pe.wait_ge(chunk_copied, done + 4)
                key_scores(0, lambda g: PQT1[:, g, :], PKT1)
                pe.wait_ge(routed, 3 + b)

        @block.vector
        def _(dve):
            steps = [0]
            V = nc.vector

            def link(ins):
                steps[0] += 1
                ins.then_inc(vec_step, 1)
                dve.wait_ge(vec_step, steps[0])

            V.memset(max8[:, :], 0.0).then_inc(ring_free, RING)
            V.memset(wgt[:, :], 0.0).then_inc(chunk_added, 2)

            dve.wait_ge(small_loaded, 80)
            link(V.tensor_copy(pos_f[:, :], pos_i[:, :]))
            V.tensor_copy(sinks[:, :].rearrange("p (g o e) -> p g o e", o=2, e=2),
                          sinks_in[:, :].rearrange("p (g e o) -> p g o e", o=2, e=2))
            for i in range(HALF_ROT):
                inv = float(np.float32(ROPE_THETA) ** np.float32(-i * 2.0 / (2 * HALF_ROT)))
                last = V.tensor_scalar(ang[:, :, i], pos_f[:, :], inv, None, ALU.mult)
            link(last)
            magic = 1.5 * 2.0 ** 23
            c1 = 6.28125
            c2 = round((2 * np.pi - c1) * 2.0 ** 20) / 2.0 ** 20
            c3 = float(np.float32(2 * np.pi - c1 - c2))
            link(V.tensor_scalar(turns[:, :, :], ang[:, :, :], float(1 / (2 * np.pi)), magic, ALU.mult, ALU.add))
            link(V.tensor_scalar(turns[:, :, :], turns[:, :, :], magic, None, ALU.subtract))
            for c in (c1, c2, c3):
                link(V.scalar_tensor_tensor(out=ang[:, :, :], in0=turns[:, :, :], scalar=-c, in1=ang[:, :, :],
                                            op0=ALU.mult, op1=ALU.add))
            V.tensor_scalar(ang[:, :, :], ang[:, :, :], 3.1415925, -3.1415925, ALU.min, ALU.max).then_inc(angles_ready, 1)
            dve.wait_ge(sines_ready, 1)
            link(V.tensor_tensor(cosT[:, :, :], cosT[:, :, :], cosT[:, :, :], ALU.mult))
            link(V.tensor_scalar(cosT[:, :, :], cosT[:, :, :], -2.0, 1.0, ALU.mult, ALU.add))

            def inverse_root(bs, width, summed, n_sum, var, root, n):
                st = [stat[:, i, bs] for i in range(6)]
                dve.wait_ge(summed, n_sum)
                link(V.tensor_scalar(st[1], st[0], 1.0 / width, EPS, ALU.mult, ALU.add))
                V.reciprocal(st[2], st[1]).then_inc(var, 1)
                dve.wait_ge(root, n)
                link(V.tensor_tensor(st[4], st[3], st[3], ALU.mult))
                link(V.tensor_tensor(st[4], st[4], st[1], ALU.mult))
                link(V.tensor_scalar(st[4], st[4], -0.5, 1.5, ALU.mult, ALU.add))
                link(V.tensor_tensor(st[5], st[3], st[4], ALU.mult))

            def norm(n):
                blocks = NORMS[n][1]
                inverse_root(slice(blocks[0], blocks[-1] + 1), D, sq_done, norm_before(n + 1), var_ready,
                             root_ready, n + 1)
                if n:
                    dve.wait_ge(gain_loaded, 16 * n)
                for b in blocks:
                    V.scalar_tensor_tensor(out=H[:, b, :], in0=X[:, b, :], scalar=stat[:, 5, b:b + 1],
                                           in1=gain[:, :], op0=ALU.mult, op1=ALU.mult).then_inc(h_ready, 1)
                dve.wait_ge(h_ready, norm_before(n + 1))

            def rope(v, cos, sin, tmp):
                _, blocks, heads, dim = v.shape
                half = dim // 8
                a, b_ = v[:, :, :, 0:half], v[:, :, :, half:2 * half]
                step = HALF_ROT // half
                shape = [P, blocks, heads, half]
                cs = cos[:, :, 0:HALF_ROT:step].unsqueeze(2).broadcast_to(shape)
                sn = sin[:, :, 0:HALF_ROT:step].unsqueeze(2).broadcast_to(shape)
                t = [tmp[:, i, 0:blocks * heads * half].rearrange("p (b h d) -> p b h d", b=blocks, h=heads)
                     for i in range(4)]
                V.tensor_tensor(t[0], a, cs, ALU.mult)
                V.tensor_tensor(t[1], b_, sn, ALU.mult)
                V.tensor_tensor(t[2], b_, cs, ALU.mult)
                link(V.tensor_tensor(t[3], a, sn, ALU.mult))
                V.tensor_tensor(a, t[0], t[1], ALU.subtract)
                link(V.tensor_tensor(b_, t[2], t[3], ALU.add))

            def mask_scores(layer, q):
                pr, g, nk = q % 2, q % 4, (q % 8) // 4 + 1
                dve.wait_ge(sc_done, q + 1)
                if layer == 1 or q >= 2:
                    dve.wait_ge(pt_done, q - 1 + layer)
                    dve.wait_ge(prob_ready, q - 1 + layer)
                src = ps[:, 0:1024].rearrange("p (h k) -> p h k", h=4)[:, :, 0:nk * P]
                mask = (band[:, T - nk * P:T], keep[:, 0:nk * P])[layer]
                s = SC[layer][pr][:, :, 0:nk * P]
                link(V.scalar_tensor_tensor(out=s, in0=src, scalar=float((64, P)[layer]) ** -0.5,
                                            in1=mask.unsqueeze(1).broadcast_to([P, 4, nk * P]),
                                            op0=ALU.mult, op1=ALU.add))
                link(V.reduce_max(soft[:, pr, 4, :], s, AX.X))
                if layer == 0:
                    hs = sinks[:, 4 * g:4 * g + 4]
                    link(V.tensor_tensor(soft[:, pr, 4, :], soft[:, pr, 4, :], hs, ALU.max))
                    V.tensor_tensor(soft[:, pr, 2, :], hs, soft[:, pr, 4, :], ALU.subtract)
                V.tensor_scalar(soft[:, pr, 0, :], soft[:, pr, 4, :], -1.0, None, ALU.mult).then_inc(sc_read, 1)

            def normalise(layer, q):
                pr, nk = q % 2, (q % 8) // 4 + 1
                dve.wait_ge(exp_done, q + 1)
                den = soft[:, pr, 1, :]
                if layer == 0:
                    link(V.tensor_tensor(den, den, soft[:, pr, 3, :], ALU.add))
                link(V.reciprocal(soft[:, pr, 5, :], den))
                s = SC[layer][pr][:, :, 0:nk * P]
                V.tensor_tensor(s, s, soft[:, pr, 5, :].unsqueeze(2).broadcast_to([P, 4, nk * P]),
                                ALU.mult).then_inc(prob_ready, 1)

            def route(layer, b):
                dve.wait_ge(rs_done, layer * NB + b + 1)
                at = (1 - layer) * b * 2048
                s = ps[:, at:at + 2048].rearrange("p (g n) -> p g n", n=NKEY)
                rest = MTf[:, 0:2048].rearrange("p (g n) -> p g n", n=NKEY)
                G = 2 * PEER_H

                def top16(groups, vals, idxs, src, left):
                    for g in range(groups):
                        last = V.max(vals[:, g, 0:8], src[:, g, :])
                    link(last)
                    yield
                    for g in range(groups):
                        last = V.max_index(idxs[:, g, 0:8], vals[:, g, 0:8], src[:, g, :])
                    yield
                    for g in range(groups):
                        last = V.match_replace(left[:, g, :], vals[:, g, 0:8], src[:, g, :], TAKEN)
                    link(last)
                    yield
                    for g in range(groups):
                        last = V.max(vals[:, g, 8:16], left[:, g, :])
                    link(last)
                    yield
                    for g in range(groups):
                        last = V.max_index(idxs[:, g, 8:16], vals[:, g, 8:16], left[:, g, :])
                    link(last)

                yield from top16(G, top_s, top_i, s, rest)
                yield
                grid = [P, PEER_H, PEER_K, PEER_K]
                ts = top_s[:, :, :].rearrange("p (h c) k -> p h c k", c=2)
                ti = top_i[:, :, :].rearrange("p (h c) k -> p h c k", c=2)
                cand = MTf[:, 2048:4096]
                link(V.tensor_tensor(cand.rearrange("p (h a b) -> p h a b", a=PEER_K, b=PEER_K),
                                     ts[:, :, 0, :].unsqueeze(3).broadcast_to(grid),
                                     ts[:, :, 1, :].unsqueeze(2).broadcast_to(grid), ALU.add))
                spare = PR[:, 6144:8192]
                yield from top16(PEER_H, best_s, best_j, cand.rearrange("p (h n) -> p h n", h=PEER_H),
                                 spare.rearrange("p (h n) -> p h n", h=PEER_H))
                yield
                gt = gate[:, b, :].rearrange("p (h k) -> p h k", k=PEER_K)
                V.tensor_tensor(gt, best_s[:, :, :], best_s[:, :, 0:1].broadcast_to([P, PEER_H, PEER_K]),
                                ALU.subtract).then_inc(best_ready, 1)
                bj = best_j[:, :, :].rearrange("p h k -> p (h k)")
                V.tensor_single_scalar(half_j[:, 0, :], bj, 4, ALU.logical_shift_right)
                link(V.tensor_single_scalar(half_j[:, 1, :], bj, 15, ALU.bitwise_and))
                for c in range(2):
                    if c:
                        yield
                    hot = MTf[:, 0:2048]
                    link(V.tensor_tensor(hot.rearrange("p (s a) -> p s a", a=PEER_K),
                                         half_j[:, c, :].unsqueeze(2).broadcast_to([P, SLOTS, PEER_K]),
                                         iota16[:, :].unsqueeze(1).broadcast_to([P, SLOTS, PEER_K]), ALU.is_equal))
                    link(V.tensor_tensor(spare.rearrange("p (h k a) -> p h k a", k=PEER_K, a=PEER_K),
                                         hot.rearrange("p (h k a) -> p h k a", k=PEER_K, a=PEER_K),
                                         ti[:, :, c, :].unsqueeze(2).broadcast_to(grid), ALU.mult))
                    link(V.reduce_sum(half_i[:, c, :], spare.rearrange("p (s a) -> p s a", a=PEER_K), AX.X))
                link(V.scalar_tensor_tensor(out=eidx[:, b, :], in0=half_i[:, 0, :], scalar=float(NKEY),
                                            in1=half_i[:, 1, :], op0=ALU.mult, op1=ALU.add))
                yield
                dve.wait_ge(gexp_done, layer * NB + b + 1)
                link(V.reduce_sum(gsum[:, 0, :], gt, AX.X))
                link(V.reciprocal(gsum[:, 1, :], gsum[:, 0, :]))
                V.tensor_tensor(gt, gt, gsum[:, 1, :].unsqueeze(2).broadcast_to([P, PEER_H, PEER_K]),
                                ALU.mult).then_inc(routed, 1)
                dve.wait_ge(routed, layer * NB + b + 1)

            def dot(b, phase, i, s, to):
                dve.wait_ge(ring_free, i * PEER_K + (phase * SLOTS + s + RING))
                dve.wait_ge(landed[s % RING], i * 32 + 16 * (phase * SLOTS // RING + s // RING + 1))
                V.tensor_tensor_reduce(out=junk, in0=ring[:, s % RING, :], in1=H[:, b, :], scale=1.0, scalar=0.0,
                                       op0=ALU.mult, op1=ALU.add, accum_out=to).then_inc(ring_free, 1)

            def weigh(b, phase, i, s, weight):
                dve.wait_ge(ring_free, i * PEER_K + (phase * SLOTS + s + RING))
                dve.wait_ge(landed[s % RING], i * 32 + 16 * (phase * SLOTS // RING + s // RING + 1))
                V.scalar_tensor_tensor(out=X[:, b, :], in0=ring[:, s % RING, :], scalar=weight, in1=X[:, b, :],
                                       op0=ALU.mult, op1=ALU.add).then_inc(ring_free, 1)

            def expert_dots(layer, b, phase, between=None):
                o = layer * NB + b
                if between:
                    for n in range(SLOTS):
                        dot(b, phase, n // PEER_K, n % PEER_K, dots[:, n:n + 1])
                        if n % 4 == 3:
                            between(n // 4)
                else:
                    with dve.Fori(0, PEER_H) as i:
                        for s in range(PEER_K):
                            if s == 0:
                                dve.wait_ge(dots_saved, i + 1)
                                dve.nop(nofuse=True)
                            dot(b, phase, i, s, dots16[:, s:s + 1])
                        dve.wait_ge(ring_free, i * PEER_K + (phase * SLOTS + PEER_K + RING))
                        V.tensor_copy(dots[:, bass.ds(i * PEER_K, PEER_K)], dots16[:, :]).then_inc(dots_saved, 1)
                    dve.wait_ge(dots_saved, PEER_H + 1)
                dve.wait_ge(ring_free, (phase + 1) * SLOTS + RING)
                V.tensor_copy(wgt[:, 0:1], dots[:, 0:1]).then_inc(dots_ready, 1)
                dve.wait_ge(gelu_ready, o + 1)
                link(V.tensor_tensor(wgt[:, :], gelu[:, :], gate[:, b, :], ALU.mult))

            def expert_sum(b, phase, between=None):
                if between:
                    for n in range(SLOTS):
                        weigh(b, phase, n // PEER_K, n % PEER_K, wgt[:, n:n + 1])
                        if n % 4 == 3:
                            between(n // 4)
                else:
                    with dve.Fori(0, PEER_H) as i:
                        for s in range(PEER_K):
                            weigh(b, phase, i, s, wgt[:, bass.ds(i * PEER_K + s, 1)])
                dve.wait_ge(ring_free, (phase + 1) * SLOTS + RING)

            V.memset(dots16[:, :], 0.0).then_inc(dots_saved, 1)
            norm(0)
            dve.wait_ge(chunk_copied, 3)
            rope(QKV[:, :, 0:1280].rearrange("p b (h d) -> p b h d", d=64), cosT[:, :, :], sinT[:, :, :], rope_tmp0)
            kd = kdup[:, :].rearrange("p (b g n) -> p b g n", b=NB, g=4)
            for b in range(NB):
                for c in range(2):
                    last = V.tensor_copy(kd[:, b, :, c * 64:(c + 1) * 64],
                                         QKV[:, b, 1024:1280].rearrange("p (g d) -> p g d", g=4))
            last.then_inc(roped, 1)
            dve.wait_ge(consts_ready, 1)
            mask_scores(0, 0)
            for q in range(8):
                if q < 7:
                    mask_scores(0, q + 1)
                normalise(0, q)
            m0 = chunk_before("out0")
            with dve.Fori(0, 2) as i:
                for c in range(2):
                    dve.wait_ge(chunk_done, i * 2 + (m0 + c + 1))
                    for b in range(NB):
                        cols = X[:, b, bass.ds(i * 1024 + c * CH, CH)]
                        last = V.tensor_tensor(cols, bank(4 * ((m0 + c) % 2) + b), cols, ALU.add)
                    last.then_inc(chunk_added, 1)
            dve.wait_ge(chunk_added, 2 + 4)
            norm(1)
            for _ in route(0, 0):
                pass

            def index_group(b, g):
                n = (b + 1) * P
                dve.wait_ge(ix_done, 4 * b + g + 1)
                src = ps[:, (g % 2) * 1024:(g % 2 + 1) * 1024].rearrange("p (h k) -> p h k", h=4)[:, :, 0:n]
                V.scalar_tensor_tensor(out=IXL[:, :, 0:n], in0=src, scalar=0.0,
                                       in1=iw[:, b, 4 * g:4 * g + 4].unsqueeze(2).broadcast_to([P, 4, n]),
                                       op0=ALU.max, op1=ALU.mult).then_inc(ix_read, 1)
                dve.wait_ge(ix_read, 4 * b + g + 1)
                link(V.reduce_sum((ixsum if g else score)[:, 0:n], IXL[:, :, 0:n].rearrange("p h k -> p k h"), AX.X))
                if g:
                    link(V.tensor_tensor(score[:, 0:n], score[:, 0:n], ixsum[:, 0:n], ALU.add))

            def mix_pieces(b):
                norm(2 + 2 * b)
                yield
                inverse_root(slice(b, b + 1), Q_RANK, cq_sq, b + 1, cq_var, cq_root, b + 1)
                V.scalar_tensor_tensor(out=C1[:, 0:CH], in0=C1[:, 0:CH], scalar=stat[:, 5, b:b + 1],
                                       in1=gain_q[:, :], op0=ALU.mult, op1=ALU.mult).then_inc(cq_ready, 1)
                yield
                cs, sn = cosT[:, b:b + 1, :], sinT[:, b:b + 1, :]
                dve.wait_ge(chunk_copied, copied_before("uq", b) + 6)

                def heads(v, dim):
                    return v.rearrange("p (b h d) -> p b h d", b=1, d=dim)

                rope(heads(UQ[:, 0:2048], P), cs, sn, rope_tmp1)
                yield
                rope(heads(UQ[:, 2048:3072], 64), cs, sn, rope_tmp1)
                rope(heads(C1[:, 512:640], P), cs, sn, rope_tmp1)
                rope(heads(C1[:, 768:832], 64), cs, sn, rope_tmp1)
                for c in range(2):
                    V.tensor_copy(ikdup[:, c * 64:(c + 1) * 64], C1[:, 768:832])
                V.tensor_scalar(iw[:, b, :].rearrange("p (g o e) -> p g o e", o=2, e=2),
                                C1[:, 832:848].rearrange("p (g e o) -> p g o e", o=2, e=2),
                                float(HEADS) ** -0.5 * 64.0 ** -0.5, None, ALU.mult).then_inc(roped, 1)
                dve.wait_ge(roped, 2 + b)
                yield
                for g in range(4):
                    index_group(b, g)
                    if g == 1:
                        yield
                yield
                n = (b + 1) * P
                link(V.tensor_tensor(score[:, n - P:n], score[:, n - P:n], band[:, P:T], ALU.add))
                for r in range(TOPK_KEYS // 8):
                    link(V.max(max8[:, :], score[:, 0:n]))
                    link(V.match_replace(score[:, 0:n], max8[:, :], score[:, 0:n], TAKEN))
                    if r == 3:
                        yield
                link(V.tensor_scalar(keep[:, 0:n], score[:, 0:n], TAKEN / 2, NEG, ALU.is_gt, ALU.mult))
                link(V.tensor_tensor(keep[:, n - P:n], keep[:, n - P:n], band[:, P:T], ALU.add))
                for q in range(8 + 4 * b, 12 + 4 * b):
                    yield
                    mask_scores(1, q)
                    yield
                    normalise(1, q)

            def out_pieces(b):
                m0 = chunk_before("out1", b)
                for c in range(4):
                    dve.wait_ge(chunk_done, m0 + c + 1)
                    cols = X[:, b, c * CH:(c + 1) * CH]
                    V.tensor_tensor(cols, bank(4 * ((m0 + c) % 2)), cols, ALU.add).then_inc(chunk_added, 1)
                    yield
                dve.wait_ge(chunk_added, 2 + 4 * (b + 2))
                norm(3 + 2 * b)
                yield
                yield from route(1, b)

            def block_pieces(b):
                yield from mix_pieces(b)
                yield
                yield from out_pieces(b)

            def paced(pieces, at, finish=True):
                def between(place):
                    if place in at:
                        next(pieces, None)
                    if finish and place == SLOTS // 4 - 1:
                        for _ in pieces:
                            pass
                return between

            MIX_AT = (0, 6, 11, 12) + tuple(range(14, 26)) + (30,)
            OUT_AT = (1, 3, 5, 6) + tuple(range(16, 29))
            expert_dots(0, 0, 0, paced(route(0, 1), range(1, 27, 2)))
            expert_sum(0, 1)
            for b in range(NB):
                pieces = block_pieces(b)
                expert_dots(b, 1 - b, 2 + 2 * b, paced(pieces, MIX_AT, finish=False))
                expert_sum(1 - b, 3 + 2 * b, paced(pieces, OUT_AT))
            expert_dots(1, 1, 6)
            expert_sum(1, 7)
            norm(6)


NAMES = ["x", "positions", "norm_mix0", "w_in0", "sinks0", "conv_w0", "w_out0", "norm_ffn0", "peer_wq0",
         "peer_keys0", "peer_u0", "peer_v0", "norm_mix1", "w_in1", "g_qa1", "w_uq1", "w_out1", "norm_ffn1",
         "peer_wq1", "peer_keys1", "peer_u1", "peer_v1", "norm_final"]


def kernel(**inputs):
    import concourse.bacc as _bacc
    from concourse.bass_utils import run_bass_kernel_spmd as _run

    nc = _bacc.Bacc("TRN2", target_bir_lowering=False, num_devices=1)
    arrays, args = {}, []
    for name in NAMES:
        a = np.ascontiguousarray(inputs[name])
        arrays[f"in_{name}"] = a
        args.append(nc.dram_tensor(f"in_{name}", a.shape, mybir.dt.from_np(a.dtype), kind="ExternalInput").ap())
    args.append(nc.dram_tensor("out", (1, T, D), mybir.dt.float32, kind="ExternalOutput").ap())
    program(nc, *args)
    r = _run(nc, [arrays], core_ids=[0])
    return r.results[0]["out"]
```

```python
from contextlib import ExitStack

import numpy as np

import concourse.bass as bass
from concourse import mybir

P = 128
D = 2048
T = 256
NB = T // P
KT_ = D // P
CH = 512
EPS = 1e-5
NEG = -1e30
TAKEN = -3e38
ROPE_THETA = 500000.0
HALF_ROT = 16
CONV_COLS = 1024
Q_RANK = 512
IN1_COLS = 848
TOPK_KEYS = 64
HEADS = 16
PEER_H = 8
PEER_K = 16
NKEY = 128
SLOTS = PEER_H * PEER_K
RING = 8
WSLOTS = 4

TRANSPOSES = [("h0", 0, 8), ("qk0", 0, 6), ("keys0", 0, 4), ("h1", 0, 4), ("h1", 1, 4)] + [
    (name, b, n) for b in (0, 1) for name, n in (("h2", 4), ("cq", 1), ("qk1", 7), ("keys1", 4), ("h3", 4))]
LARGE = [("in0_qkv", 0, 6, 3), ("in0_conv", 0, 12, 0), ("out0", 0, 8, 4)]
SMALL = [("wq0", 0, 16, 4), ("out0", 1, 16, 4), ("wq0", 1, 16, 4)] + [
    (name, b, tiles, chunks) for b in (0, 1)
    for name, tiles, chunks in (("in1", 8, 2), ("uq", 6, 6), ("out1", 16, 4), ("wq1", 16, 4))]
CONV_ORDER = (2, 3, 4, 5, 0, 1)
HALVES = 2 * len(CONV_ORDER)
CONV_BESIDE = [(2, 3), (4, 5), (6,), (7,), (8,), (9,), (10,), (11,)]
NORMS = [(0, (0, 1)), (1, (0,)), (1, (1,)), (2, (0,)), (3, (0,)), (2, (1,)), (3, (1,)),
         (4, (0,)), (4, (1,))]

HEAD_OF_PLACE = [(0, 2, 1, 3), (0, 1, 2, 3)]


def ahead(table, name, b):
    return table[:[row[:2] for row in table].index((name, b))]


def tr_before(name, b=0):
    return sum(row[2] for row in ahead(TRANSPOSES, name, b))


def tiles_before(name, b=0):
    return sum(row[2] for row in ahead(LARGE if (name, b) in [r[:2] for r in LARGE] else SMALL, name, b))


def chunk_before(name, b=0):
    return sum(row[3] for row in ahead(LARGE + SMALL, name, b))


def copied_before(name, b=0):
    return sum(row[3] for row in ahead(LARGE + SMALL, name, b) if not row[0].startswith("out"))


def added_before(name, b=0):
    return 2 + sum(row[3] for row in ahead(LARGE + SMALL, name, b) if row[0].startswith("out"))


def gains_loaded(n):
    return 1 + sum(NORMS[i][0] != NORMS[i - 1][0] for i in range(1, n + 1))


def norm_before(n):
    return sum(len(blocks) for _, blocks in NORMS[:n])


def program(nc, x, positions, norm_mix0, w_in0, sinks0, conv_w0, w_out0, norm_ffn0, peer_wq0,
            peer_keys0, peer_u0, peer_v0, norm_mix1, w_in1, g_qa1, w_uq1, w_out1, norm_ffn1,
            peer_wq1, peer_keys1, peer_u1, peer_v1, norm_final, out):
    fp32 = mybir.dt.float32
    bf16 = mybir.dt.bfloat16
    u32 = mybir.dt.uint32
    i32 = mybir.dt.int32
    ALU = mybir.AluOpType
    ACT = mybir.ActivationFunctionType
    AX = mybir.AxisListType
    ctx = ExitStack()
    with ctx:
        def sb(name, shape, dt=fp32):
            return ctx.enter_context(nc.sbuf_tensor(name, shape, dt))

        def sem(name):
            return ctx.enter_context(nc.semaphore(name))

        X = sb("X", [P, NB, D])
        H = sb("H", [P, NB, D])
        HT = sb("HT", [P, KT_, T])
        MT = sb("MT", [P, KT_, T])
        PR = sb("PR", [P, 9216])
        A = sb("A", [P, 4096])
        ring = sb("ring", [P, RING, D])
        gain = sb("gain", [P, D])
        gain_q = sb("gain_q", [P, Q_RANK])
        kdup = sb("kdup", [P, 1024])
        KT = sb("KT", [P, 1024])
        ident = sb("ident", [P, P])
        band = sb("band", [P, T])
        keep = sb("keep", [P, T])
        VB = sb("VB", [P, NB, P])
        ikdup = sb("ikdup", [P, P])
        iota16 = sb("iota16", [P, PEER_K])
        sinks_in = sb("sinks_in", [P, HEADS])
        sinks = sb("sinks", [P, HEADS])
        conv_w = sb("conv_w", [P, 3, 8])
        pos_i = sb("pos_i", [P, NB], i32)
        pos_f = sb("pos_f", [P, NB])
        cosT = sb("cosT", [P, NB, HALF_ROT])
        sinT = sb("sinT", [P, NB, HALF_ROT])
        ang = sb("ang", [P, NB, HALF_ROT])
        turns = sb("turns", [P, NB, HALF_ROT])
        stat = sb("stat", [P, 8, NB])
        soft = sb("soft", [P, 2, 6, 4])
        iw = sb("iw", [P, NB, HEADS])
        score = sb("score", [P, T])
        max8 = sb("max8", [P, 8])
        gsum = sb("gsum", [P, 2, PEER_H])
        gate = sb("gate", [P, NB, SLOTS])
        eidx = sb("eidx", [P, NB, SLOTS], u32)
        cur = sb("cur", [P, 2, 8], u32)
        dots16 = sb("dots16", [P, PEER_K])
        dots = sb("dots", [P, SLOTS])
        wgt = sb("wgt", [P, SLOTS])
        ps = ctx.enter_context(nc.psum_tensor("ps", [P, 8 * 512], fp32))

        def flat(t):
            return t[:, :, :].rearrange("p a b -> p (a b)")

        Hf, MTf = flat(H), flat(MT)
        QKV = PR[:, 0:3072].rearrange("p (b n) -> p b n", b=NB)
        GATES = PR[:, 3072:9216].rearrange("p (g t) -> p g t", t=T)
        PKT0 = PR[:, 4096:6144].rearrange("p (g n) -> p g n", n=NKEY)
        PKN0 = Hf[:, 2048:4096].rearrange("p (g n) -> p g n", n=NKEY)
        C1, UQ = PR[:, 0:IN1_COLS], PR[:, IN1_COLS:IN1_COLS + 3072]
        PQT = PR[:, 0:2048].rearrange("p (g t) -> p g t", t=P)
        PKT1 = PR[:, 2048:4096].rearrange("p (g n) -> p g n", n=NKEY)
        IQT = PR[:, 8192:9216].rearrange("p (g t) -> p g t", t=P)
        HTf = flat(HT)
        HT1 = HTf[:, 0:2048].rearrange("p (k t) -> p k t", t=P)
        QT1 = HTf[:, 2048:4096].rearrange("p (h t) -> p h t", t=P)
        PKN1 = QT1
        MTB = MTf.rearrange("p (b k t) -> p b k t", b=NB, t=P)
        MT1 = MTB[:, 0, :, :]
        QT0 = Hf[:, 2048:4096].rearrange("p (k t) -> p k t", t=T)
        rope_tmp0 = Hf[:, 0:2048].rearrange("p (k n) -> p k n", k=4)
        rope_tmp1 = MTf[:, 1024:2048].rearrange("p (k n) -> p k n", k=4)
        SC = [[A[:, 0:1024], A[:, 1024:2048]], [A[:, 0:1024]] * 2]
        PT = [[A[:, 2048:3072], A[:, 3072:4096]], [A[:, 1024:2048]] * 2]
        SC, PT = ([[t.rearrange("p (h k) -> p h k", h=4) for t in pair] for pair in both] for both in (SC, PT))
        IXL = A[:, 0:1024].rearrange("p (h k) -> p h k", h=4)
        ixsum = A[:, 1024:1024 + T]
        junk = kdup[:, :].bitcast(bf16)
        def inA(at, groups, n):
            return A[:, at:at + groups * n].rearrange("p (g n) -> p g n", n=n)

        top_s, top_i = inA(0, 2 * PEER_H, PEER_K), inA(256, 2 * PEER_H, PEER_K).bitcast(u32)
        best_s, best_j = inA(512, PEER_H, PEER_K), inA(640, PEER_H, PEER_K).bitcast(u32)
        gelu = A[:, 1280:1280 + SLOTS]
        half_j, half_i = inA(768, 2, SLOTS).bitcast(u32), inA(1024, 2, SLOTS)
        wring = ring[:, :, :].rearrange("p (s two) n -> p s (two n)", two=2)

        def wtile(slot):
            return wring[:, slot, :].rearrange("p (k n) -> p k n", n=CH)

        def small(t):
            return t.rearrange("p (k n) -> p k n", n=CH)

        tiles_l0 = [small(t) for t in (PR[:, 2048:4096], PR[:, 6144:8192], A[:, 2048:4096], HTf[:, 2048:4096])]
        tiles_l1 = [small(t) for t in (PR[:, 4096:6144], PR[:, 6144:8192], A[:, 2048:4096], MTf[:, 2048:4096])]

        def bank(i, n=1, w=512):
            return ps[:, i * 512:(i + n - 1) * 512 + w]

        x_loaded, gain_loaded, small_loaded = sem("x_loaded"), sem("gain_loaded"), sem("small_loaded")
        keys_loaded, out_stored = sem("keys_loaded"), sem("out_stored")
        w_loaded = [sem(f"w_loaded{i}") for i in range(WSLOTS)]
        w_used = sem("w_used")
        s_loaded = [sem(f"s_loaded{i}") for i in range(WSLOTS)]
        s_used = sem("s_used")
        keys1_loaded = sem("keys1_loaded")
        consts_ready = sem("consts_ready")
        conv_done = sem("conv_done")
        angles_ready, sines_ready = sem("angles_ready"), sem("sines_ready")
        sq_done, var_ready, root_ready, h_ready = (sem("sq_done"), sem("var_ready"),
                                                   sem("root_ready"), sem("h_ready"))
        cq_sq, cq_var, cq_root, cq_ready = sem("cq_sq"), sem("cq_var"), sem("cq_root"), sem("cq_ready")
        tr_done, tr_copied = sem("tr_done"), sem("tr_copied")
        chunk_done, chunk_copied, chunk_added = sem("chunk_done"), sem("chunk_copied"), sem("chunk_added")
        half_done, half_copied = sem("half_done"), sem("half_copied")
        roped = sem("roped")
        ix_done, ix_read = sem("ix_done"), sem("ix_read")
        sc_done, sc_read, exp_done, prob_ready = (sem("sc_done"), sem("sc_read"), sem("exp_done"),
                                                  sem("prob_ready"))
        pt_done, pt_copied, pv_done, pv_copied = (sem("pt_done"), sem("pt_copied"), sem("pv_done"),
                                                  sem("pv_copied"))
        rs_done, best_ready, gexp_done, routed = (sem("rs_done"), sem("best_ready"),
                                                  sem("gexp_done"), sem("routed"))
        part_read = sem("part_read")
        heads_routed = sem("heads_routed")
        idx_cur = sem("idx_cur")
        landed = [sem(f"landed{i}") for i in range(RING)]
        ring_free = sem("ring_free")
        dots_saved, dots_ready, gelu_ready = sem("dots_saved"), sem("dots_ready"), sem("gelu_ready")
        vec_step, act_step, pool_step = sem("vec_step"), sem("act_step"), sem("pool_step")

        gains = [norm_mix0, norm_ffn0, norm_mix1, norm_ffn1, norm_final]
        keys_dram = [peer_keys0, peer_keys1]
        u_dram, v_dram = [peer_u0, peer_u1], [peer_v0, peer_v1]

        def transposes(stage, b=0):
            def pack(srcs, dst):
                return [(srcs[i:i + 4], dst(i)) for i in range(0, len(srcs), 4)]

            def cols(t, n, at=0):
                return [t[:, at + k * P:at + (k + 1) * P] for k in range(n)]

            if stage == "h0":
                return [e for c in range(NB) for e in pack(
                    cols(H[:, c, :], KT_), lambda i, c=c: HT[:, i:i + 4, c * P:(c + 1) * P])]
            if stage in ("h1", "h2", "h3"):
                return pack(cols(H[:, b, :], KT_), lambda i: HT1[:, i:i + 4, :])
            if stage == "keys0":
                return pack([PKN0[:, g, :] for g in range(2 * PEER_H)], lambda i: PKT0[:, i:i + 4, :])
            if stage == "keys1":
                return pack([PKN1[:, g, :] for g in range(2 * PEER_H)], lambda i: PKT1[:, i:i + 4, :])
            if stage == "cq":
                return pack(cols(C1, Q_RANK // P), lambda i: MT1[:, i:i + 4, :])
            if stage == "qk0":
                kd = kdup[:, :].rearrange("p (b g n) -> p b g n", b=NB, g=4)
                kt = KT[:, :].rearrange("p (g t) -> p g t", g=4)
                return [e for c in range(NB) for e in
                        pack(cols(QKV[:, c, :], 8), lambda i, c=c: QT0[:, i:i + 4, c * P:(c + 1) * P])
                        + pack([kd[:, c, g, :] for g in range(4)],
                               lambda i, c=c: kt[:, :, c * P:(c + 1) * P])]
            kt = KT[:, 0:2 * T].rearrange("p (g t) -> p g t", g=2)
            return (pack(cols(UQ, HEADS), lambda i: QT1[:, i:i + 4, :])
                    + pack(cols(UQ, 8, 2048), lambda i: IQT[:, i:i + 4, :])
                    + pack([C1[:, 512:640], ikdup[:, :]], lambda i: kt[:, :, b * P:(b + 1) * P]))

        block = ctx.enter_context(nc.Block())

        @block.sync
        def _(sp):
            def load_qkv_tile(n):
                sp.dma_start(wtile(n % WSLOTS), w_in0.rearrange("(h k p) n -> h p k n", h=2, p=P)
                             [n % 2][:, :, (n // 2) * CH:(n // 2 + 1) * CH]).then_inc(w_loaded[n % WSLOTS], 16)

            sp.dma_start(X[:, 0, :], x[0, 0:P, :]).then_inc(x_loaded, 16)
            sp.dma_start(gain[:, :], gains[0].partition_broadcast(P)).then_inc(gain_loaded, 16)
            sp.dma_start(X[:, 1, :], x[0, P:T, :]).then_inc(x_loaded, 16)
            load_qkv_tile(0)
            load_qkv_tile(1)
            with nc.allow_non_contiguous_dma(reason="a few small vectors laid over the partitions"):
                sp.dma_start(pos_i[:, :], positions.rearrange("o (b p) -> p (o b)", p=P)).then_inc(small_loaded, 16)
            sp.dma_start(sinks_in[:, :], sinks0.partition_broadcast(P)).then_inc(small_loaded, 16)
            with nc.allow_non_contiguous_dma(reason="a few small vectors laid over the partitions"):
                sp.dma_start(conv_w[:, :, :], conv_w0.rearrange("w (c p) -> p w c", p=P)).then_inc(small_loaded, 16)
            sp.dma_start(gain_q[:, :], g_qa1.partition_broadcast(P)).then_inc(small_loaded, 16)

            def load_chunks(n0, w, c0, chunks):
                w = w.rearrange("(h k p) n -> h p k n", h=2, p=P)
                with sp.Fori(0, chunks // 2) as i:
                    for c in range(2):
                        for h in range(2):
                            n = n0 + 2 * c + h
                            sp.wait_ge(w_used, i * 4 + (n - WSLOTS + 1))
                            sp.dma_start(wtile(n % WSLOTS), w[h][:, :, bass.ds((i * 2 + (c0 + c)) * CH, CH)]
                                         ).then_inc(w_loaded[n % WSLOTS], 16)

            def load_gain(n):
                sp.wait_ge(h_ready, norm_before(n))
                sp.dma_start(gain[:, :], gains[NORMS[n][0]].partition_broadcast(P)).then_inc(gain_loaded, 16)

            for n in range(2, 6):
                if n >= WSLOTS:
                    sp.wait_ge(w_used, n - WSLOTS + 1)
                load_qkv_tile(n)
            load_gain(1)
            n0 = tiles_before("in0_conv")
            load_chunks(n0, w_in0, 3 + CONV_ORDER[0], 4)
            load_chunks(n0 + 8, w_in0, 3 + CONV_ORDER[4], 2)
            load_chunks(tiles_before("out0"), w_out0, 0, 4)

            def load_quarters(name, b, w, tiles):
                w = w.rearrange("(q k p) n -> q p k n", q=4, p=P)
                n0 = tiles_before(name, b)
                with sp.Fori(0, 4) as i:
                    for q in range(4):
                        slot = (n0 + q) % WSLOTS
                        sp.wait_ge(s_used, i * 4 + (n0 + q + 1))
                        sp.dma_start(tiles[slot], w[q][:, :, bass.ds(i * CH, CH)]).then_inc(s_loaded[slot], 16)

            sp.wait_ge(w_used, tiles_before("out0"))
            sp.wait_ge(pv_done, 8)
            sp.wait_ge(conv_done, 1)
            load_quarters("wq0", 0, peer_wq0, tiles_l0)
            load_quarters("out0", 1, w_out0, tiles_l0)
            load_quarters("wq0", 1, peer_wq0, tiles_l0)
            for b in range(NB):
                sp.wait_ge(routed, b + 2)
                load_gain(3 + 2 * b)
                n = tiles_before("in1", b)
                w = w_in1.rearrange("(q k p) n -> q p k n", q=4, p=P)
                for c, width in enumerate((CH, IN1_COLS - CH)):
                    for q in range(4):
                        sp.wait_ge(s_used, n + 1)
                        sp.dma_start(tiles_l1[n % WSLOTS][:, :, 0:width], w[q][:, :, c * CH:c * CH + width]
                                     ).then_inc(s_loaded[n % WSLOTS], 16)
                        n += 1
                load_gain(4 + 2 * b)
                w = w_uq1.rearrange("(k p) n -> p k n", p=P)
                for c in range(6):
                    sp.wait_ge(s_used, n + 1)
                    sp.dma_start(tiles_l1[n % WSLOTS], w[:, :, c * CH:(c + 1) * CH]).then_inc(s_loaded[n % WSLOTS], 16)
                    n += 1
                load_quarters("out1", b, w_out1, tiles_l1)
                sp.wait_ge(pv_done, 8 + 4 * (b + 1))
                sp.dma_start(PKN1, peer_keys1.rearrange("h c n d -> n (h c) d")).then_inc(keys1_loaded, 16)
                load_quarters("wq1", b, peer_wq1, tiles_l1)
            load_gain(7)
            for b in range(NB):
                sp.wait_ge(h_ready, norm_before(8 + b))
                sp.dma_start(out[0, b * P:(b + 1) * P, :], H[:, b, :]).then_inc(out_stored, 16)
            sp.wait_ge(out_stored, 16 * NB)

        @block.gpsimd
        def _(pool):
            steps = [0]

            def link(ins):
                steps[0] += 1
                ins.then_inc(pool_step, 1)
                pool.wait_ge(pool_step, steps[0])

            nc.gpsimd.iota(iota16[:, :], pattern=[[1, PEER_K]], base=0, channel_multiplier=0,
                           allow_small_or_imprecise_dtypes=True)
            nc.gpsimd.memset(ident[:, :], 0.0)
            link(nc.gpsimd.memset(band[:, :], 0.0))
            nc.gpsimd.affine_select(out=ident[:, :], in_=ident[:, :], compare_op=ALU.not_equal, fill=1.0,
                                    base=0, pattern=[[-1, P]], channel_multiplier=1)
            nc.gpsimd.affine_select(out=band[:, 0:P], in_=band[:, 0:P], compare_op=ALU.is_gt, fill=NEG,
                                    base=0, pattern=[[1, P]], channel_multiplier=-1)
            nc.gpsimd.affine_select(out=band[:, P:T], in_=band[:, P:T], compare_op=ALU.is_ge, fill=NEG,
                                    base=0, pattern=[[-1, P]], channel_multiplier=1).then_inc(consts_ready, 1)

            bg, cg, hx = (GATES[:, 8 * i:8 * i + 8, :] for i in range(3))
            tmp = Hf[:, 0:2048].rearrange("p (g t) -> p g t", t=T)

            def tap(w):
                return conv_w[:, w, :].unsqueeze(2).broadcast_to([P, 8, T])

            pool.wait_ge(small_loaded, 64)
            pool.wait_ge(half_copied, 8)
            link(nc.gpsimd.tensor_tensor(cg, cg, hx, ALU.mult))
            nc.gpsimd.tensor_tensor(hx, cg, tap(2), ALU.mult)
            link(nc.gpsimd.tensor_tensor(tmp, cg, tap(1), ALU.mult))
            link(nc.gpsimd.tensor_tensor(hx[:, :, 1:T], hx[:, :, 1:T], tmp[:, :, 0:T - 1], ALU.add))
            link(nc.gpsimd.tensor_tensor(tmp, cg, tap(0), ALU.mult))
            link(nc.gpsimd.tensor_tensor(hx[:, :, 2:T], hx[:, :, 2:T], tmp[:, :, 0:T - 2], ALU.add))
            pool.wait_ge(half_copied, HALVES)
            hx, bg = (t.rearrange("p g (b t) -> p g b t", b=NB) for t in (hx, bg))
            nc.gpsimd.tensor_tensor(MTB[:, :, 8:16, :].rearrange("p b g t -> p g b t"), hx, bg,
                                    ALU.mult).then_inc(conv_done, 1)

            pool.wait_ge(pv_done, 8)
            pool.wait_ge(conv_done, 1)
            pool.dma_start(PKN0, peer_keys0.rearrange("h c n d -> n (h c) d")).then_inc(keys_loaded, 16)

            def gather(layer, b, table, phase):
                with pool.Fori(0, PEER_H) as i:
                    if phase == 0:
                        pool.wait_ge(heads_routed, i + 1)
                        pool.nop(nofuse=True)
                    for o in range(2):
                        nc.gpsimd.tensor_copy(cur[:, o, :], eidx[:, b, bass.ds(i * 16 + o * 8, 8)]).then_inc(idx_cur, 1)
                        pool.wait_ge(idx_cur, i * 2 + (phase * 16 + o + 1))
                        pool.nop(nofuse=True)
                        for r in range(RING):
                            pool.wait_ge(ring_free, i * 16 + (phase * SLOTS + o * 8 + r + 1))
                            pool.nop(nofuse=True)
                            pool.indirect_dma_start(ring[:, r, :], None, table,
                                                    bass.IndirectOffsetOnAxis(cur[:, o, r:r + 1], 0)).then_inc(landed[r], 16)

            pool.wait_ge(w_used, sum(row[2] for row in LARGE))
            for layer in range(2):
                for b in range(NB):
                    if layer or b:
                        pool.wait_ge(routed, layer * NB + b + 1)
                    gather(layer, b, u_dram[layer], layer * 4 + b * 2)
                    gather(layer, b, v_dram[layer], layer * 4 + b * 2 + 1)

        @block.scalar
        def _(act):
            steps = [0]

            def link(ins):
                steps[0] += 1
                ins.then_inc(act_step, 1)
                act.wait_ge(act_step, steps[0])

            def squares(n):
                for b in NORMS[n][1]:
                    nc.scalar.activation(H[:, b, :], X[:, b, :], ACT.Square,
                                         accum_out=stat[:, 0, b:b + 1]).then_inc(sq_done, 1)
                act.wait_ge(var_ready, n + 1)
                bs = slice(NORMS[n][1][0], NORMS[n][1][-1] + 1)
                nc.scalar.activation(stat[:, 3, bs], stat[:, 2, bs], ACT.Sqrt).then_inc(root_ready, 1)

            def copy_transposes(stage, b=0):
                n0 = tr_before(stage, b)
                for n, (srcs, dst) in enumerate(transposes(stage, b)):
                    act.wait_ge(tr_done, n0 + n + 1)
                    nc.scalar.copy(dst, bank(n, w=len(srcs) * P).rearrange("p (g n) -> p g n", n=P)).then_inc(tr_copied, 1)

            def copy_queries(name, b):
                m0 = chunk_before(name, b)
                with act.Fori(0, 2) as i:
                    for c in range(2):
                        act.wait_ge(chunk_done, i * 2 + (m0 + c + 1))
                        src = bank(4 * ((m0 + c) % 2), 4).rearrange("p (g n) -> p g n", n=512)[:, :, 0:P]
                        nc.scalar.copy(PQT[:, bass.ds(i * 8 + c * 4, 4), :], src).then_inc(chunk_copied, 1)

            def exps(layer, q):
                act.wait_ge(sc_read, q + 1)
                pr, nk = q % 2, (q % 8) // 4 + 1
                s = SC[layer][pr]
                for h in range(4):
                    last = nc.scalar.activation(s[:, h, 0:nk * P], s[:, h, 0:nk * P], ACT.Exp,
                                                bias=soft[:, pr, 0, h:h + 1], accum_out=soft[:, pr, 1, h:h + 1])
                if layer == 0:
                    last = nc.scalar.activation(soft[:, pr, 3, :], soft[:, pr, 2, :], ACT.Exp)
                last.then_inc(exp_done, 1)

            def copy_out(layer, q):
                pr, b, g, nk = q % 2, (q % 8) // 4, q % 4, (q % 8) // 4 + 1
                act.wait_ge(pt_done, q + 1)
                if layer == 1 or q >= 2:
                    act.wait_ge(pv_done, q - 1 + layer)
                src = bank(2, 2).rearrange("p (h n) -> p h n", h=4)[:, :, 0:nk * P]
                nc.scalar.copy(PT[layer][pr][:, :, 0:nk * P], src).then_inc(pt_copied, 1)
                act.wait_ge(pv_done, q + 1)
                n = (2, 4)[layer]
                dst = MT1[:, 4 * g:4 * g + 4, :] if layer else MTB[:, b, 2 * g:2 * g + 2, :]
                nc.scalar.copy(dst, bank(4 + pr, w=n * P).rearrange("p (h n) -> p h n", h=n)).then_inc(pv_copied, 1)

            def gate_exp(layer, b):
                act.wait_ge(best_ready, layer * NB + b + 1)
                nc.scalar.activation(gate[:, b, :], gate[:, b, :], ACT.Exp).then_inc(gexp_done, 1)

            def gelus(layer, b):
                act.wait_ge(dots_ready, layer * NB + b + 1)
                nc.scalar.activation(gelu[:, :], dots[:, :], ACT.Gelu).then_inc(gelu_ready, 1)

            act.wait_ge(x_loaded, 32)
            squares(0)
            copy_transposes("h0")
            act.wait_ge(angles_ready, 1)
            nc.scalar.activation(sinT[:, :, :], ang[:, :, :], ACT.Sin)
            nc.scalar.activation(cosT[:, :, :], ang[:, :, :], ACT.Sin, scale=0.5).then_inc(sines_ready, 1)
            for c in range(3):
                act.wait_ge(chunk_done, c + 1)
                for b in range(NB):
                    last = nc.scalar.copy(QKV[:, b, c * CH:(c + 1) * CH], bank(4 * (c % 2) + b))
                last.then_inc(chunk_copied, 1)

            def copy_half(n):
                act.wait_ge(half_done, n + 1)
                g = 4 * CONV_ORDER[n // 2] + 2 * (n % 2)
                nc.scalar.copy(GATES[:, g:g + 2, :], bank(6 + n % 2).rearrange("p (g t) -> p g t", t=T)
                               ).then_inc(half_copied, 1)

            copy_half(0)
            copy_half(1)
            copy_transposes("qk0")
            exps(0, 0)
            for q in range(8):
                if q < 7:
                    exps(0, q + 1)
                for n in CONV_BESIDE[q]:
                    copy_half(n)
                copy_out(0, q)
            for b in range(NB):
                act.wait_ge(chunk_added, added_before("out0", b) + 4)
                squares(1 + b)
                if b == 0:
                    copy_transposes("keys0")
                copy_transposes("h1", b)
                copy_queries("wq0", b)
                if b:
                    gelus(0, 0)
                gate_exp(0, b)

            def copy_token_chunk(m, dst, width=CH):
                act.wait_ge(chunk_done, m + 1)
                nc.scalar.copy(dst, bank(4 * (m % 2), w=width)).then_inc(chunk_copied, 1)

            for b in range(NB):
                act.wait_ge(ring_free, RING + 2 * SLOTS * (b + 1))
                squares(3 + 2 * b)
                copy_transposes("h2", b)
                m0 = chunk_before("in1", b)
                copy_token_chunk(m0, C1[:, 0:CH])
                act.wait_ge(chunk_done, m0 + 2)
                nc.scalar.copy(VB[:, b, :], bank(4 * ((m0 + 1) % 2))[:, P:2 * P])
                copy_token_chunk(m0 + 1, C1[:, CH:IN1_COLS], IN1_COLS - CH)
                act.wait_ge(chunk_copied, copied_before("uq", b))
                nc.scalar.activation(A[:, 0:CH], C1[:, 0:CH], ACT.Square,
                                     accum_out=stat[:, 0, b:b + 1]).then_inc(cq_sq, 1)
                act.wait_ge(cq_var, b + 1)
                nc.scalar.activation(stat[:, 3, b:b + 1], stat[:, 2, b:b + 1], ACT.Sqrt).then_inc(cq_root, 1)
                copy_transposes("cq", b)
                m0 = chunk_before("uq", b)
                for c in range(6):
                    copy_token_chunk(m0 + c, UQ[:, c * CH:(c + 1) * CH])
                copy_transposes("qk1", b)
                for q in range(8 + 4 * b, 12 + 4 * b):
                    exps(1, q)
                    copy_out(1, q)
                gelus(b, 1 - b)
                copy_transposes("keys1", b)
                act.wait_ge(chunk_added, added_before("out1", b) + 4)
                squares(4 + 2 * b)
                copy_transposes("h3", b)
                copy_queries("wq1", b)
                gate_exp(1, b)
            act.wait_ge(ring_free, RING + 6 * SLOTS)
            squares(7)
            gelus(1, 1)
            act.wait_ge(ring_free, RING + 8 * SLOTS)
            squares(8)

        @block.tensor
        def _(pe):
            def transpose_stage(stage, b=0):
                n0 = tr_before(stage, b)
                banks = transposes(stage, b)
                for n, (srcs, dst) in enumerate(banks):
                    for i, s in enumerate(srcs):
                        last = nc.tensor.transpose(ps[:, n * 512 + i * P:n * 512 + (i + 1) * P], s, ident[:, :])
                    last.then_inc(tr_done, 1)
                pe.wait_ge(tr_copied, n0 + len(banks))

            def chunk_ends(used, count):
                pe.wait_ge(used, count)
                pe.nop(nofuse=True).then_inc(chunk_done, 1)

            def chunk_tile(m, tile, lhs, k0, count, width=CH, tokens=None):
                for k in range(tile.shape[1]):
                    kk = k0 + k
                    flags = dict(start=(kk == 0), stop=(kk == count - 1))
                    if tokens:
                        for g in range(4):
                            last = nc.tensor.matmul(bank(4 * (m % 2) + g, w=tokens), tile[:, k, g * P:(g + 1) * P],
                                                    lhs[:, kk, :], **flags)
                    else:
                        for b in range(lhs.shape[2] // P):
                            last = nc.tensor.matmul(bank(4 * (m % 2) + b, w=width), lhs[:, kk, b * P:(b + 1) * P],
                                                    tile[:, k, 0:width], **flags)
                return last

            def conv_half(n):
                n0 = tiles_before("in0_conv") + n // 2 * 2
                if n >= 2:
                    pe.wait_ge(half_copied, n - 1)
                for g in (0, 1):
                    at = (6 + n % 2) * 512 + g * T
                    for t in range(2):
                        slot = (n0 + t) % WSLOTS
                        pe.wait_ge(w_loaded[slot], 16 * ((n0 + t) // WSLOTS + 1))
                        for k in range(8):
                            c = (n % 2 * 2 + g) * P
                            last = nc.tensor.matmul(ps[:, at:at + T], wtile(slot)[:, k, c:c + P], HT[:, 8 * t + k, :],
                                                    start=(t == k == 0), stop=(t == 1 and k == 7))
                        if n % 2 and g:
                            last.then_inc(w_used, 1)
                if n % 2:
                    pe.wait_ge(w_used, n0 + 2)
                    pe.nop(nofuse=True).then_inc(half_done, 1)
                else:
                    last.then_inc(half_done, 1)

            def out0_loop():
                n0, m0, done = tiles_before("out0"), chunk_before("out0"), added_before("out0")
                with pe.Fori(0, 2) as i:
                    for c in range(2):
                        pe.wait_ge(chunk_added, i * 2 + (done + c - 1))
                        for t in range(2):
                            n = n0 + 2 * c + t
                            if t:
                                pe.wait_ge(conv_done, 1)
                            pe.wait_ge(w_loaded[n % WSLOTS], i * 16 + 16 * (n // WSLOTS + 1))
                            chunk_tile(m0 + c, wtile(n % WSLOTS), MTB[:, 0, :, :], 8 * t, KT_).then_inc(w_used, 1)
                        chunk_ends(w_used, i * 4 + (n0 + 2 * c + 2))

            def small_loop(name, b, tiles, lhs, tokens, drained, d0):
                n0, m0 = tiles_before(name, b), chunk_before(name, b)
                with pe.Fori(0, 2) as i:
                    for c in range(2):
                        pe.wait_ge(drained, i * 2 + (d0 + c - 1))
                        for t in range(4):
                            n = n0 + 4 * c + t
                            pe.wait_ge(s_loaded[n % WSLOTS], i * 32 + 16 * (n // WSLOTS + 1))
                            chunk_tile(m0 + c, tiles[n % WSLOTS], lhs, 4 * t, KT_, tokens=tokens).then_inc(s_used, 1)
                        chunk_ends(s_used, i * 8 + (WSLOTS + n0 + 4 * c + 4))

            def scores(layer, q):
                pr, b, g, nk = q % 2, (q % 8) // 4, q % 4, (q % 8) // 4 + 1
                if q % 8:
                    pe.wait_ge(sc_read, q)
                for i in range(4):
                    h = 4 * g + HEAD_OF_PLACE[layer][i]
                    o = ps[:, i * T:i * T + nk * P]
                    if layer == 0:
                        r = 64 * (h % 2)
                        lhs = QT0[r:r + 64, h // 2, b * P:(b + 1) * P]
                        rhs = KT[r:r + 64, g * T:g * T + nk * P]
                    else:
                        lhs, rhs = QT1[:, h, :], KT[:, 0:nk * P]
                    last = nc.tensor.matmul(o, lhs, rhs, start=True, stop=True)
                last.then_inc(sc_done, 1)

            def values(layer, q):
                pr, b, g, nk = q % 2, (q % 8) // 4, q % 4, (q % 8) // 4 + 1
                pe.wait_ge(prob_ready, q + 1)
                if q >= 1:
                    pe.wait_ge(pt_copied, q)
                for i in range(4):
                    for kb in range(nk):
                        last = nc.tensor.transpose(ps[:, 1024 + i * T + kb * P:1024 + i * T + (kb + 1) * P],
                                                   SC[layer][pr][:, i, kb * P:(kb + 1) * P], ident[:, :])
                last.then_inc(pt_done, 1)
                pe.wait_ge(pt_copied, q + 1)
                if q >= 2:
                    pe.wait_ge(pv_copied, q - 1)
                for i in range(4):
                    h = 4 * g + HEAD_OF_PLACE[layer][i]
                    for kb in range(nk):
                        if layer == 0:
                            r = 64 * (h % 2)
                            c = (4 + pr) * 512 + (h % 4 // 2) * P
                            o = ps[r:r + 64, c:c + P]
                            lhs = QKV[:, kb, 1280 + g * 64:1280 + (g + 1) * 64]
                        else:
                            o = ps[:, (4 + pr) * 512 + i * P:(4 + pr) * 512 + (i + 1) * P]
                            lhs = VB[:, kb, :]
                        last = nc.tensor.matmul(o, lhs, PT[layer][pr][:, i, kb * P:(kb + 1) * P],
                                                start=(kb == 0), stop=(kb == nk - 1))
                last.then_inc(pv_done, 1)

            def attention(layer, q0, n):
                scores(layer, q0)
                for q in range(q0, q0 + n):
                    if q + 1 < q0 + n:
                        scores(layer, q + 1)
                    if layer == 0:
                        for half in CONV_BESIDE[q]:
                            conv_half(half)
                    values(layer, q)
                pe.wait_ge(pv_copied, q0 + n)

            def key_scores(keys, count):
                for g in range(2 * PEER_H):
                    last = nc.tensor.matmul(ps[:, g * NKEY:(g + 1) * NKEY], PQT[:, g, :], keys[:, g, :],
                                            start=True, stop=True)
                last.then_inc(rs_done, 1)
                pe.wait_ge(routed, count)

            def queries_and_scores():
                n, m0, c0 = tiles_before("wq0", 0), chunk_before("wq0"), copied_before("wq0")
                for c in range(4):
                    if c >= 2:
                        pe.wait_ge(part_read, c - 1)
                    for t in range(4):
                        pe.wait_ge(s_loaded[n % WSLOTS], 16 * (n // WSLOTS + 1))
                        chunk_tile(m0 + c, tiles_l0[n % WSLOTS], HT1, 4 * t, KT_, tokens=P).then_inc(s_used, 1)
                        n += 1
                    chunk_ends(s_used, WSLOTS + n)
                    pe.wait_ge(chunk_copied, c0 + c + 1)
                    for g in range(4):
                        at = 2048 * ((m0 + c) % 2) + g * NKEY
                        last = nc.tensor.matmul(ps[:, at:at + NKEY], PQT[:, 4 * c + g, :], PKT0[:, 4 * c + g, :],
                                                start=True, stop=True)
                    last.then_inc(rs_done, 1)
                pe.wait_ge(part_read, 4)

            pe.nop(nofuse=True).then_inc(s_used, WSLOTS)
            pe.wait_ge(consts_ready, 1)
            pe.wait_ge(h_ready, 2)
            transpose_stage("h0")
            for c in range(3):
                if c >= 2:
                    pe.wait_ge(chunk_copied, c - 1)
                for t in range(2):
                    n = 2 * c + t
                    pe.wait_ge(w_loaded[n % WSLOTS], 16 * (n // WSLOTS + 1))
                    chunk_tile(c, wtile(n % WSLOTS), HT, 8 * t, KT_).then_inc(w_used, 1)
                chunk_ends(w_used, 2 * c + 2)
            pe.wait_ge(chunk_copied, 3)
            conv_half(0)
            conv_half(1)
            pe.wait_ge(roped, 1)
            transpose_stage("qk0")
            attention(0, 0, 8)
            out0_loop()
            pe.wait_ge(keys_loaded, 16)
            pe.wait_ge(chunk_added, added_before("out0") + 4)
            transpose_stage("keys0")
            pe.wait_ge(h_ready, norm_before(2))
            transpose_stage("h1", 0)
            queries_and_scores()
            small_loop("out0", 1, tiles_l0, MTB[:, 1, :, :], None, chunk_added, added_before("out0", 1))
            pe.wait_ge(chunk_added, added_before("out0", 1) + 4)
            pe.wait_ge(h_ready, norm_before(3))
            transpose_stage("h1", 1)
            small_loop("wq0", 1, tiles_l0, HT1, P, chunk_copied, copied_before("wq0", 1))
            pe.wait_ge(chunk_copied, copied_before("wq0", 1) + 4)
            key_scores(PKT0, 2)

            for b in range(NB):
                n, m, done = tiles_before("in1", b), chunk_before("in1", b), copied_before("in1", b)
                pe.wait_ge(h_ready, norm_before(4 + 2 * b))
                transpose_stage("h2", b)
                for c, width in enumerate((CH, IN1_COLS - CH)):
                    for t in range(4):
                        pe.wait_ge(s_loaded[n % WSLOTS], 16 * (n // WSLOTS + 1))
                        chunk_tile(m + c, tiles_l1[n % WSLOTS], HT1, 4 * t, KT_, width).then_inc(s_used, 1)
                        n += 1
                    chunk_ends(s_used, WSLOTS + n)
                pe.wait_ge(cq_ready, b + 1)
                pe.wait_ge(chunk_copied, done + 2)
                transpose_stage("cq", b)
                m, done = chunk_before("uq", b), copied_before("uq", b)
                for c in range(6):
                    if c >= 2:
                        pe.wait_ge(chunk_copied, done + c - 1)
                    pe.wait_ge(s_loaded[n % WSLOTS], 16 * (n // WSLOTS + 1))
                    chunk_tile(m + c, tiles_l1[n % WSLOTS], MT1, 0, 4).then_inc(s_used, 1)
                    n += 1
                    chunk_ends(s_used, WSLOTS + n)
                pe.wait_ge(chunk_copied, done + 6)
                pe.wait_ge(roped, 2 + b)
                transpose_stage("qk1", b)
                for g in range(4):
                    if g >= 2:
                        pe.wait_ge(ix_read, 4 * b + g - 1)
                    for i in range(4):
                        h = 4 * g + HEAD_OF_PLACE[0][i]
                        r = 64 * (h % 2)
                        at = (g % 2) * 1024 + i * T
                        last = nc.tensor.matmul(ps[:, at:at + (b + 1) * P], IQT[r:r + 64, h // 2, :],
                                                KT[r:r + 64, T:T + (b + 1) * P], start=True, stop=True)
                    last.then_inc(ix_done, 1)
                pe.wait_ge(ix_read, 4 * b + 4)
                attention(1, 8 + 4 * b, 4)
                small_loop("out1", b, tiles_l1, MT1, None, chunk_added, added_before("out1", b))
                pe.wait_ge(keys1_loaded, 16 * (b + 1))
                pe.wait_ge(chunk_added, added_before("out1", b) + 4)
                transpose_stage("keys1", b)
                pe.wait_ge(h_ready, norm_before(5 + 2 * b))
                transpose_stage("h3", b)
                done = copied_before("wq1", b)
                small_loop("wq1", b, tiles_l1, HT1, P, chunk_copied, done)
                pe.wait_ge(chunk_copied, done + 4)
                key_scores(PKT1, 3 + b)

        @block.vector
        def _(dve):
            steps = [0]
            V = nc.vector

            def link(ins):
                steps[0] += 1
                ins.then_inc(vec_step, 1)
                dve.wait_ge(vec_step, steps[0])

            V.memset(max8[:, :], 0.0).then_inc(ring_free, RING)
            V.memset(wgt[:, :], 0.0).then_inc(chunk_added, 2)

            def inverse_root(bs, width, summed, n_sum, var, root, n):
                st = [stat[:, i, bs] for i in range(6)]
                dve.wait_ge(summed, n_sum)
                link(V.tensor_scalar(st[1], st[0], 1.0 / width, EPS, ALU.mult, ALU.add))
                V.reciprocal(st[2], st[1]).then_inc(var, 1)
                dve.wait_ge(root, n)
                link(V.tensor_tensor(st[4], st[3], st[3], ALU.mult))
                link(V.tensor_tensor(st[4], st[4], st[1], ALU.mult))
                link(V.tensor_scalar(st[4], st[4], -0.5, 1.5, ALU.mult, ALU.add))
                link(V.tensor_tensor(st[5], st[3], st[4], ALU.mult))

            def norm(n):
                blocks = NORMS[n][1]
                inverse_root(slice(blocks[0], blocks[-1] + 1), D, sq_done, norm_before(n + 1), var_ready,
                             root_ready, n + 1)
                dve.wait_ge(gain_loaded, 16 * gains_loaded(n))
                for b in blocks:
                    V.scalar_tensor_tensor(out=H[:, b, :], in0=X[:, b, :], scalar=stat[:, 5, b:b + 1],
                                           in1=gain[:, :], op0=ALU.mult, op1=ALU.mult).then_inc(h_ready, 1)
                dve.wait_ge(h_ready, norm_before(n + 1))

            def rope(v, cos, sin, tmp):
                _, blocks, heads, dim = v.shape
                half = dim // 8
                a, b_ = v[:, :, :, 0:half], v[:, :, :, half:2 * half]
                step = HALF_ROT // half
                shape = [P, blocks, heads, half]
                cs = cos[:, :, 0:HALF_ROT:step].unsqueeze(2).broadcast_to(shape)
                sn = sin[:, :, 0:HALF_ROT:step].unsqueeze(2).broadcast_to(shape)
                t = [tmp[:, i, 0:blocks * heads * half].rearrange("p (b h d) -> p b h d", b=blocks, h=heads)
                     for i in range(4)]
                V.tensor_tensor(t[0], a, cs, ALU.mult)
                V.tensor_tensor(t[1], b_, sn, ALU.mult)
                V.tensor_tensor(t[2], b_, cs, ALU.mult)
                link(V.tensor_tensor(t[3], a, sn, ALU.mult))
                V.tensor_tensor(a, t[0], t[1], ALU.subtract)
                link(V.tensor_tensor(b_, t[2], t[3], ALU.add))

            def mask_scores(layer, q):
                pr, g, nk = q % 2, q % 4, (q % 8) // 4 + 1
                dve.wait_ge(sc_done, q + 1)
                if layer == 1 or q >= 2:
                    dve.wait_ge(pt_done, q - 1 + layer)
                    dve.wait_ge(prob_ready, q - 1 + layer)
                src = ps[:, 0:1024].rearrange("p (h k) -> p h k", h=4)[:, :, 0:nk * P]
                mask = (band[:, T - nk * P:T], keep[:, 0:nk * P])[layer]
                s = SC[layer][pr][:, :, 0:nk * P]
                link(V.scalar_tensor_tensor(out=s, in0=src, scalar=float((64, P)[layer]) ** -0.5,
                                            in1=mask.unsqueeze(1).broadcast_to([P, 4, nk * P]),
                                            op0=ALU.mult, op1=ALU.add))
                link(V.reduce_max(soft[:, pr, 4, :], s, AX.X))
                if layer == 0:
                    hs = sinks[:, 4 * g:4 * g + 4]
                    link(V.tensor_tensor(soft[:, pr, 4, :], soft[:, pr, 4, :], hs, ALU.max))
                    V.tensor_tensor(soft[:, pr, 2, :], hs, soft[:, pr, 4, :], ALU.subtract)
                V.tensor_scalar(soft[:, pr, 0, :], soft[:, pr, 4, :], -1.0, None, ALU.mult).then_inc(sc_read, 1)

            def normalise(layer, q):
                pr, nk = q % 2, (q % 8) // 4 + 1
                dve.wait_ge(exp_done, q + 1)
                den = soft[:, pr, 1, :]
                if layer == 0:
                    link(V.tensor_tensor(den, den, soft[:, pr, 3, :], ALU.add))
                link(V.reciprocal(soft[:, pr, 5, :], den))
                s = SC[layer][pr][:, :, 0:nk * P]
                V.tensor_tensor(s, s, soft[:, pr, 5, :].unsqueeze(2).broadcast_to([P, 4, nk * P]),
                                ALU.mult).then_inc(prob_ready, 1)

            def top16(groups, vals, idxs, src, left, read=None):
                for g in range(groups):
                    last = V.max(vals[:, g, 0:8], src[:, g, :])
                link(last)
                yield
                for g in range(groups):
                    last = V.max_index(idxs[:, g, 0:8], vals[:, g, 0:8], src[:, g, :])
                yield
                for g in range(groups):
                    last = V.match_replace(left[:, g, :], vals[:, g, 0:8], src[:, g, :], TAKEN)
                if read:
                    last.then_inc(part_read, 1)
                    dve.wait_ge(part_read, read)
                else:
                    link(last)
                yield
                for g in range(groups):
                    last = V.max(vals[:, g, 8:16], left[:, g, :])
                link(last)
                yield
                for g in range(groups):
                    last = V.max_index(idxs[:, g, 8:16], vals[:, g, 8:16], left[:, g, :])
                link(last)

            def experts(b, h0, heads, s, rest, cand, spare, hot, first=False, read=None):
                hs, slots = slice(h0, h0 + heads), slice(h0 * PEER_K, (h0 + heads) * PEER_K)
                n = heads * PEER_K
                g0, G = 2 * h0, 2 * heads
                yield from top16(G, top_s[:, g0:g0 + G, :], top_i[:, g0:g0 + G, :], s, rest, read)
                yield
                grid = [P, heads, PEER_K, PEER_K]
                ts = top_s[:, g0:g0 + G, :].rearrange("p (h c) k -> p h c k", c=2)
                ti = top_i[:, g0:g0 + G, :].rearrange("p (h c) k -> p h c k", c=2)
                link(V.tensor_tensor(cand.rearrange("p (h a b) -> p h a b", a=PEER_K, b=PEER_K),
                                     ts[:, :, 0, :].unsqueeze(3).broadcast_to(grid),
                                     ts[:, :, 1, :].unsqueeze(2).broadcast_to(grid), ALU.add))
                yield from top16(heads, best_s[:, hs, :], best_j[:, hs, :], cand.rearrange("p (h n) -> p h n", h=heads),
                                 spare.rearrange("p (h n) -> p h n", h=heads))
                yield
                if h0 + heads == PEER_H:
                    gt = gate[:, b, :].rearrange("p (h k) -> p h k", k=PEER_K)
                    V.tensor_tensor(gt, best_s[:, :, :], best_s[:, :, 0:1].broadcast_to([P, PEER_H, PEER_K]),
                                    ALU.subtract).then_inc(best_ready, 1)
                bj = best_j[:, hs, :].rearrange("p h k -> p (h k)")
                V.tensor_single_scalar(half_j[:, 0, slots], bj, 4, ALU.logical_shift_right)
                link(V.tensor_single_scalar(half_j[:, 1, slots], bj, 15, ALU.bitwise_and))
                for c in range(2):
                    if c:
                        yield
                    link(V.tensor_tensor(hot.rearrange("p (s a) -> p s a", a=PEER_K),
                                         half_j[:, c, slots].unsqueeze(2).broadcast_to([P, n, PEER_K]),
                                         iota16[:, :].unsqueeze(1).broadcast_to([P, n, PEER_K]), ALU.is_equal))
                    link(V.tensor_tensor(spare.rearrange("p (h k a) -> p h k a", k=PEER_K, a=PEER_K),
                                         hot.rearrange("p (h k a) -> p h k a", k=PEER_K, a=PEER_K),
                                         ti[:, :, c, :].unsqueeze(2).broadcast_to(grid), ALU.mult))
                    link(V.reduce_sum(half_i[:, c, slots], spare.rearrange("p (s a) -> p s a", a=PEER_K), AX.X))
                last = V.scalar_tensor_tensor(out=eidx[:, b, slots], in0=half_i[:, 0, slots], scalar=float(NKEY),
                                              in1=half_i[:, 1, slots], op0=ALU.mult, op1=ALU.add)
                if first:
                    last.then_inc(heads_routed, heads)
                else:
                    link(last)

            def gates(layer, b):
                gt = gate[:, b, :].rearrange("p (h k) -> p h k", k=PEER_K)
                dve.wait_ge(gexp_done, layer * NB + b + 1)
                link(V.reduce_sum(gsum[:, 0, :], gt, AX.X))
                link(V.reciprocal(gsum[:, 1, :], gsum[:, 0, :]))
                V.tensor_tensor(gt, gt, gsum[:, 1, :].unsqueeze(2).broadcast_to([P, PEER_H, PEER_K]),
                                ALU.mult).then_inc(routed, 1)
                dve.wait_ge(routed, layer * NB + b + 1)

            def route(layer, b):
                dve.wait_ge(rs_done, layer * NB + b + 4)
                s = ps[:, 0:2048].rearrange("p (g n) -> p g n", n=NKEY)
                rest = MTf[:, 0:2048]
                yield from experts(b, 0, PEER_H, s, rest.rearrange("p (g n) -> p g n", n=NKEY),
                                   MTf[:, 2048:4096], PR[:, 6144:8192], rest)
                yield
                gates(layer, b)

            def first_route(c):
                dve.wait_ge(rs_done, c + 1)
                s = bank(4 * ((chunk_before("wq0") + c) % 2)).rearrange("p (g n) -> p g n", n=NKEY)
                rest, *scratch = (MTf[:, i * CH:(i + 1) * CH] for i in range(4))
                rest = rest.rearrange("p (g n) -> p g n", n=NKEY)
                if c == 0:
                    for h in range(2):
                        g = slice(2 * h, 2 * h + 2)
                        yield from experts(0, h, 1, s[:, g, :], rest[:, g, :], *(t[:, 0:T] for t in scratch),
                                           first=True, read=h)
                    return
                pieces = experts(0, 2 * c, 2, s, rest, *scratch, first=True, read=c + 1)
                for n in (5, 5, 3):
                    for _ in range(n):
                        next(pieces, None)
                    if n == 3 and c == 3:
                        gates(0, 0)
                    yield

            def dot(b, phase, i, s, to):
                dve.wait_ge(ring_free, i * PEER_K + (phase * SLOTS + s + RING))
                dve.wait_ge(landed[s % RING], i * 32 + 16 * (phase * SLOTS // RING + s // RING + 1))
                V.tensor_tensor_reduce(out=junk, in0=ring[:, s % RING, :], in1=H[:, b, :], scale=1.0, scalar=0.0,
                                       op0=ALU.mult, op1=ALU.add, accum_out=to).then_inc(ring_free, 1)

            def weigh(b, phase, i, s, weight):
                dve.wait_ge(ring_free, i * PEER_K + (phase * SLOTS + s + RING))
                dve.wait_ge(landed[s % RING], i * 32 + 16 * (phase * SLOTS // RING + s // RING + 1))
                V.scalar_tensor_tensor(out=X[:, b, :], in0=ring[:, s % RING, :], scalar=weight, in1=X[:, b, :],
                                       op0=ALU.mult, op1=ALU.add).then_inc(ring_free, 1)

            def expert_dots(layer, b, phase, between=None):
                o = layer * NB + b
                if between:
                    for n in range(SLOTS):
                        dot(b, phase, n // PEER_K, n % PEER_K, dots[:, n:n + 1])
                        if n % 4 == 3:
                            between(n // 4)
                else:
                    with dve.Fori(0, PEER_H) as i:
                        for s in range(PEER_K):
                            if s == 0:
                                dve.wait_ge(dots_saved, i + 1)
                                dve.nop(nofuse=True)
                            dot(b, phase, i, s, dots16[:, s:s + 1])
                        dve.wait_ge(ring_free, i * PEER_K + (phase * SLOTS + PEER_K + RING))
                        V.tensor_copy(dots[:, bass.ds(i * PEER_K, PEER_K)], dots16[:, :]).then_inc(dots_saved, 1)
                    dve.wait_ge(dots_saved, PEER_H + 1)
                dve.wait_ge(ring_free, (phase + 1) * SLOTS + RING)
                V.tensor_copy(wgt[:, 0:1], dots[:, 0:1]).then_inc(dots_ready, 1)
                dve.wait_ge(gelu_ready, o + 1)
                link(V.tensor_tensor(wgt[:, :], gelu[:, :], gate[:, b, :], ALU.mult))

            def expert_sum(b, phase, between=None):
                if between:
                    for n in range(SLOTS):
                        weigh(b, phase, n // PEER_K, n % PEER_K, wgt[:, n:n + 1])
                        if n % 4 == 3:
                            between(n // 4)
                else:
                    with dve.Fori(0, PEER_H) as i:
                        for s in range(PEER_K):
                            weigh(b, phase, i, s, wgt[:, bass.ds(i * PEER_K + s, 1)])
                dve.wait_ge(ring_free, (phase + 1) * SLOTS + RING)

            V.memset(dots16[:, :], 0.0).then_inc(dots_saved, 1)
            norm(0)

            dve.wait_ge(small_loaded, 64)
            link(V.tensor_copy(pos_f[:, :], pos_i[:, :]))
            V.tensor_copy(sinks[:, :].rearrange("p (g o e) -> p g o e", o=2, e=2),
                          sinks_in[:, :].rearrange("p (g e o) -> p g o e", o=2, e=2))
            for i in range(HALF_ROT):
                inv = float(np.float32(ROPE_THETA) ** np.float32(-i * 2.0 / (2 * HALF_ROT)))
                last = V.tensor_scalar(ang[:, :, i], pos_f[:, :], inv, None, ALU.mult)
            link(last)
            magic = 1.5 * 2.0 ** 23
            c1 = 6.28125
            c2 = round((2 * np.pi - c1) * 2.0 ** 20) / 2.0 ** 20
            c3 = float(np.float32(2 * np.pi - c1 - c2))
            link(V.tensor_scalar(turns[:, :, :], ang[:, :, :], float(1 / (2 * np.pi)), magic, ALU.mult, ALU.add))
            link(V.tensor_scalar(turns[:, :, :], turns[:, :, :], magic, None, ALU.subtract))
            for c in (c1, c2, c3):
                link(V.scalar_tensor_tensor(out=ang[:, :, :], in0=turns[:, :, :], scalar=-c, in1=ang[:, :, :],
                                            op0=ALU.mult, op1=ALU.add))
            V.tensor_scalar(ang[:, :, :], ang[:, :, :], 3.1415925, -3.1415925, ALU.min, ALU.max).then_inc(angles_ready, 1)
            dve.wait_ge(sines_ready, 1)
            link(V.tensor_tensor(cosT[:, :, :], cosT[:, :, :], cosT[:, :, :], ALU.mult))
            link(V.tensor_scalar(cosT[:, :, :], cosT[:, :, :], -2.0, 1.0, ALU.mult, ALU.add))

            dve.wait_ge(chunk_copied, 3)
            rope(QKV[:, :, 0:1280].rearrange("p b (h d) -> p b h d", d=64), cosT[:, :, :], sinT[:, :, :], rope_tmp0)
            kd = kdup[:, :].rearrange("p (b g n) -> p b g n", b=NB, g=4)
            for b in range(NB):
                for c in range(2):
                    last = V.tensor_copy(kd[:, b, :, c * 64:(c + 1) * 64],
                                         QKV[:, b, 1024:1280].rearrange("p (g d) -> p g d", g=4))
            last.then_inc(roped, 1)
            dve.wait_ge(consts_ready, 1)
            mask_scores(0, 0)
            for q in range(8):
                if q < 7:
                    mask_scores(0, q + 1)
                normalise(0, q)
            m0 = chunk_before("out0")
            with dve.Fori(0, 2) as i:
                for c in range(2):
                    dve.wait_ge(chunk_done, i * 2 + (m0 + c + 1))
                    cols = X[:, 0, bass.ds(i * 1024 + c * CH, CH)]
                    V.tensor_tensor(cols, bank(4 * ((m0 + c) % 2)), cols, ALU.add).then_inc(chunk_added, 1)
            dve.wait_ge(chunk_added, added_before("out0") + 4)
            norm(1)
            for _ in first_route(0):
                pass

            def index_group(b, g):
                n = (b + 1) * P
                dve.wait_ge(ix_done, 4 * b + g + 1)
                src = ps[:, (g % 2) * 1024:(g % 2 + 1) * 1024].rearrange("p (h k) -> p h k", h=4)[:, :, 0:n]
                V.scalar_tensor_tensor(out=IXL[:, :, 0:n], in0=src, scalar=0.0,
                                       in1=iw[:, b, 4 * g:4 * g + 4].unsqueeze(2).broadcast_to([P, 4, n]),
                                       op0=ALU.max, op1=ALU.mult).then_inc(ix_read, 1)
                dve.wait_ge(ix_read, 4 * b + g + 1)
                link(V.reduce_sum((ixsum if g else score)[:, 0:n], IXL[:, :, 0:n].rearrange("p h k -> p k h"), AX.X))
                if g:
                    link(V.tensor_tensor(score[:, 0:n], score[:, 0:n], ixsum[:, 0:n], ALU.add))

            def mix_pieces(b):
                norm(3 + 2 * b)
                yield
                inverse_root(slice(b, b + 1), Q_RANK, cq_sq, b + 1, cq_var, cq_root, b + 1)
                V.scalar_tensor_tensor(out=C1[:, 0:CH], in0=C1[:, 0:CH], scalar=stat[:, 5, b:b + 1],
                                       in1=gain_q[:, :], op0=ALU.mult, op1=ALU.mult).then_inc(cq_ready, 1)
                yield
                cs, sn = cosT[:, b:b + 1, :], sinT[:, b:b + 1, :]
                dve.wait_ge(chunk_copied, copied_before("uq", b) + 6)

                def heads(v, dim):
                    return v.rearrange("p (b h d) -> p b h d", b=1, d=dim)

                rope(heads(UQ[:, 0:2048], P), cs, sn, rope_tmp1)
                yield
                rope(heads(UQ[:, 2048:3072], 64), cs, sn, rope_tmp1)
                rope(heads(C1[:, 512:640], P), cs, sn, rope_tmp1)
                rope(heads(C1[:, 768:832], 64), cs, sn, rope_tmp1)
                for c in range(2):
                    V.tensor_copy(ikdup[:, c * 64:(c + 1) * 64], C1[:, 768:832])
                V.tensor_scalar(iw[:, b, :].rearrange("p (g o e) -> p g o e", o=2, e=2),
                                C1[:, 832:848].rearrange("p (g e o) -> p g o e", o=2, e=2),
                                float(HEADS) ** -0.5 * 64.0 ** -0.5, None, ALU.mult).then_inc(roped, 1)
                dve.wait_ge(roped, 2 + b)
                yield
                for g in range(4):
                    index_group(b, g)
                    if g == 1:
                        yield
                yield
                n = (b + 1) * P
                link(V.tensor_tensor(score[:, n - P:n], score[:, n - P:n], band[:, P:T], ALU.add))
                for r in range(TOPK_KEYS // 8):
                    link(V.max(max8[:, :], score[:, 0:n]))
                    link(V.match_replace(score[:, 0:n], max8[:, :], score[:, 0:n], TAKEN))
                    if r == 3:
                        yield
                link(V.tensor_scalar(keep[:, 0:n], score[:, 0:n], TAKEN / 2, NEG, ALU.is_gt, ALU.mult))
                link(V.tensor_tensor(keep[:, n - P:n], keep[:, n - P:n], band[:, P:T], ALU.add))
                for q in range(8 + 4 * b, 12 + 4 * b):
                    yield
                    mask_scores(1, q)
                    yield
                    normalise(1, q)

            def out_pieces(layer, b):
                m0 = chunk_before(f"out{layer}", b)
                for c in range(4):
                    dve.wait_ge(chunk_done, m0 + c + 1)
                    cols = X[:, b, c * CH:(c + 1) * CH]
                    V.tensor_tensor(cols, bank(4 * ((m0 + c) % 2)), cols, ALU.add).then_inc(chunk_added, 1)
                    yield
                dve.wait_ge(chunk_added, added_before(f"out{layer}", b) + 4)
                norm(4 + 2 * b if layer else 2)
                yield
                yield from route(layer, b)

            def block_pieces(b):
                yield from mix_pieces(b)
                yield
                yield from out_pieces(1, b)

            def paced(pieces, at, finish=True):
                def between(place):
                    if place in at:
                        next(pieces, None)
                    if finish and place == SLOTS // 4 - 1:
                        for _ in pieces:
                            pass
                return between

            MIX_AT = (0, 6, 11, 12) + tuple(range(14, 26)) + (30,)
            OUT_AT = (1, 3, 5, 6) + tuple(range(15, 21)) + (22, 23, 24, 25, 26, 28, 29)
            def first_pieces():
                for c in range(1, 4):
                    yield from first_route(c)
                yield from out_pieces(0, 1)

            pieces = first_pieces()
            expert_dots(0, 0, 0, paced(pieces, tuple(range(9)) + (12, 14, 16, 18, 19), finish=False))
            expert_sum(0, 1, paced(pieces, range(0, 26, 2)))
            for b in range(NB):
                pieces = block_pieces(b)
                expert_dots(b, 1 - b, 2 + 2 * b, paced(pieces, MIX_AT, finish=False))
                expert_sum(1 - b, 3 + 2 * b, paced(pieces, OUT_AT))
            norm(7)
            expert_dots(1, 1, 6)
            expert_sum(1, 7)
            norm(8)


NAMES = ["x", "positions", "norm_mix0", "w_in0", "sinks0", "conv_w0", "w_out0", "norm_ffn0", "peer_wq0",
         "peer_keys0", "peer_u0", "peer_v0", "norm_mix1", "w_in1", "g_qa1", "w_uq1", "w_out1", "norm_ffn1",
         "peer_wq1", "peer_keys1", "peer_u1", "peer_v1", "norm_final"]


def kernel(**inputs):
    import concourse.bacc as _bacc
    from concourse.bass_utils import run_bass_kernel_spmd as _run

    nc = _bacc.Bacc("TRN2", target_bir_lowering=False, num_devices=1)
    arrays, args = {}, []
    for name in NAMES:
        a = np.ascontiguousarray(inputs[name])
        arrays[f"in_{name}"] = a
        args.append(nc.dram_tensor(f"in_{name}", a.shape, mybir.dt.from_np(a.dtype), kind="ExternalInput").ap())
    args.append(nc.dram_tensor("out", (1, T, D), mybir.dt.float32, kind="ExternalOutput").ap())
    program(nc, *args)
    r = _run(nc, [arrays], core_ids=[0])
    return r.results[0]["out"]
```
